# Optimizing a Trainium2 kernel written in Bass

```python
import math, functools
import jax, jax.numpy as jnp
from jax import lax
import numpy as np

D_MODEL = 2048
BATCH = 1
SEQ = 512
DEPTH = 1
DEC_BATCH = 8
DEC_SEQ = 1
PAST_LEN = 256
PAGE_SIZE = 128

H_ATT = 8
DK_ATT = 64
DV_ATT = 128
H_RNN = 8
DK_RNN = 128
DV_RNN = 128
D_ATT = H_ATT * DV_ATT
D_RNN = H_RNN * DV_RNN
D_MIX = D_ATT + D_RNN
QK_ATT_W = H_ATT * 2 * DK_ATT
RNN_K_W = H_RNN * DK_RNN
IN_WIDTHS = (QK_ATT_W, QK_ATT_W, D_ATT, RNN_K_W, RNN_K_W, D_RNN, D_RNN)
D_IN = QK_ATT_W * 2 + D_ATT + RNN_K_W * 2 + D_RNN * 2
D_FF = 5632
CONV_W = 3
D_PLE = 256
ROPE_THETA = 10000.0
EPS = 1e-6
Q_BLOCK = 128
RNN_CHUNK = 16
NEG_INF = -1e30

kernel_name = "hymba_diffattn_hgrn2_convffn_step"

def rms_norm(x, gain):
    xf = x.astype(jnp.float32)
    y = xf * lax.rsqrt(jnp.mean(xf * xf, axis=-1, keepdims=True) + EPS)
    return (y * gain.astype(jnp.float32)).astype(x.dtype)

def rotary(x, pos):
    half = DK_ATT // 2
    inv_freq = 1.0 / (ROPE_THETA ** (jnp.arange(half, dtype=jnp.float32) * (2.0 / DK_ATT)))
    ang = pos.astype(jnp.float32)[:, None] * inv_freq[None, :]
    cos = jnp.cos(ang)[:, None, None, :]
    sin = jnp.sin(ang)[:, None, None, :]
    xf = x.astype(jnp.float32)
    x1, x2 = xf[..., :half], xf[..., half:]
    return jnp.concatenate([x1 * cos - x2 * sin, x2 * cos + x1 * sin], axis=-1).astype(x.dtype)

def diff_weights(s, lam):
    p = jax.nn.softmax(s, axis=-1)
    return p[:, :, 0] - lam * p[:, :, 1]

def attend_prompt(q, k, v, lam):
    B, S = q.shape[0], q.shape[1]
    nb = S // Q_BLOCK
    scale = DK_ATT ** -0.5
    qb = q.reshape(B, nb, Q_BLOCK, H_ATT, 2, DK_ATT).transpose(1, 0, 2, 3, 4, 5)
    kpos = jnp.arange(S)

    def block(args):
        qi, bi = args
        s = jnp.einsum('bqhmd,bkhmd->bhmqk', qi, k, preferred_element_type=jnp.float32) * scale
        qpos = bi * Q_BLOCK + jnp.arange(Q_BLOCK)
        s = jnp.where(kpos[None, :] <= qpos[:, None], s, NEG_INF)
        w = diff_weights(s, lam)
        return jnp.einsum('bhqk,bkhd->bqhd', w, v).astype(q.dtype)

    o = lax.map(block, (qb, jnp.arange(nb)))
    return o.transpose(1, 0, 2, 3, 4).reshape(B, S, H_ATT, DV_ATT)

def attend_sample(q, k_new, v_new, lam, k_past, v_past):
    T, P = q.shape[1], k_past.shape[1]
    scale = DK_ATT ** -0.5
    s_past = jnp.einsum('bqhmd,bkhmd->bhmqk', q, k_past, preferred_element_type=jnp.float32) * scale
    s_new = jnp.einsum('bqhmd,bkhmd->bhmqk', q, k_new, preferred_element_type=jnp.float32) * scale
    causal = jnp.tril(jnp.ones((T, T), dtype=bool))
    s_new = jnp.where(causal, s_new, NEG_INF)
    w = diff_weights(jnp.concatenate([s_past, s_new], axis=-1), lam)
    o = (jnp.einsum('bhqk,bkhd->bqhd', w[..., :P], v_past)
         + jnp.einsum('bhqk,bkhd->bqhd', w[..., P:], v_new))
    return o.astype(q.dtype)

def hgrn2_recurrence(q, k, v, log_f, s0):
    B, L = q.shape[0], q.shape[1]
    C = math.gcd(L, RNN_CHUNK)
    n = L // C

    def to_chunks(a):
        return a.astype(jnp.float32).reshape(B, n, C, H_RNN, a.shape[-1]).transpose(1, 0, 3, 2, 4)

    causal = jnp.tril(jnp.ones((C, C), dtype=bool))

    def step(S, inp):
        qc, kc, vc, gc = inp
        b = jnp.cumsum(gc, axis=-2)
        q_dec = qc * jnp.exp(b)
        a = jnp.einsum('bhtk,bhsk->bhts', q_dec, kc * jnp.exp(-b))
        a = jnp.where(causal, a, 0.0)
        o = jnp.einsum('bhts,bhsv->bhtv', a, vc) + jnp.einsum('bhtk,bhkv->bhtv', q_dec, S)
        b_last = b[:, :, -1:, :]
        S_new = (jnp.exp(b_last[:, :, 0, :])[..., None] * S
                 + jnp.einsum('bhsk,bhsv->bhkv', kc * jnp.exp(b_last - b), vc))
        return S_new, o

    S_fin, o = lax.scan(step, s0.astype(jnp.float32), (to_chunks(q), to_chunks(k), to_chunks(v), to_chunks(log_f)))
    o = o.transpose(1, 0, 3, 2, 4).reshape(B, L, H_RNN, DV_RNN)
    return o, S_fin

def conv_ffn(h, buf, w_gate, w_up, conv_w, conv_b, w_down):
    L = h.shape[1]
    g = h @ w_gate
    ext = jnp.concatenate([buf.astype(g.dtype), g], axis=1)
    c = conv_b
    for j in range(CONV_W):
        c = c + ext[:, j:j + L] * conv_w[j]
    out = (jax.nn.silu(c) * (h @ w_up)) @ w_down
    return out, ext[:, L:]

def layer_forward(x, p, pos, attend, rnn_state0, conv_buf0, lam_init, lb, wts):
    (norm_mix, w_in, q_gain, k_gain, lam_q1, lam_k1, lam_q2, lam_k2, att_gain, rnn_gain,
     w_out, norm_ffn, w_gate, w_up, conv_w, conv_b, w_down, norm_ple, w_ple_gate, w_ple_proj) = wts
    B, L = x.shape[0], x.shape[1]
    h = rms_norm(x, norm_mix)
    z = h @ w_in
    splits = [int(s) for s in np.cumsum(IN_WIDTHS)[:-1]]
    q_a, k_a, v_a, q_r, f_r, i_r, g_r = jnp.split(z, splits, axis=-1)
    q_a = rotary(rms_norm(q_a.reshape(B, L, H_ATT, 2, DK_ATT), q_gain), pos)
    k_a = rotary(rms_norm(k_a.reshape(B, L, H_ATT, 2, DK_ATT), k_gain), pos)
    v_a = v_a.reshape(B, L, H_ATT, DV_ATT)
    lam = (jnp.exp(jnp.sum(lam_q1.astype(jnp.float32) * lam_k1.astype(jnp.float32)))
           - jnp.exp(jnp.sum(lam_q2.astype(jnp.float32) * lam_k2.astype(jnp.float32))) + lam_init)
    o_att = attend(q_a, k_a, v_a, lam)
    o_att = rms_norm(o_att, att_gain) * (1.0 - lam_init)
    lbf = lb.reshape(H_RNN, DK_RNN)
    zf = f_r.astype(jnp.float32).reshape(B, L, H_RNN, DK_RNN)
    log_f = jnp.log(lbf + (1.0 - lbf) * jax.nn.sigmoid(zf))
    k_r = (1.0 - lbf) * jax.nn.sigmoid(-zf)
    o_rnn, rnn_state = hgrn2_recurrence(q_r.reshape(B, L, H_RNN, DK_RNN), k_r,
                                        i_r.reshape(B, L, H_RNN, DV_RNN), log_f, rnn_state0)
    o_rnn = rms_norm(o_rnn.astype(x.dtype), rnn_gain) * jax.nn.silu(g_r.reshape(B, L, H_RNN, DV_RNN))
    x = x + jnp.concatenate([o_att.reshape(B, L, D_ATT), o_rnn.reshape(B, L, D_RNN)], axis=-1) @ w_out
    ffn, conv_buf = conv_ffn(rms_norm(x, norm_ffn), conv_buf0, w_gate, w_up, conv_w, conv_b, w_down)
    x = x + ffn
    x = x + jax.nn.sigmoid(rms_norm(x, norm_ple) @ w_ple_gate) * (p @ w_ple_proj)
    return x, k_a.reshape(B, L, H_ATT, 2 * DK_ATT), v_a, rnn_state, conv_buf

def setup_inputs(seed: int = 0) -> dict:
    key = jax.random.key(seed)
    ks = jax.random.split(key, 40)
    n_pages = PAST_LEN // PAGE_SIZE
    n_used = DEC_BATCH * n_pages
    n_pool = (5 * n_used + 3) // 4
    f32 = jnp.float32

    def nrm(k, shape, scale=1.0):
        return jax.random.normal(k, shape, f32) * scale

    def gain(k, shape):
        return 1.0 + 0.02 * jax.random.normal(k, shape, f32)

    page_table = jax.random.permutation(ks[0], n_pool)[:n_used].reshape(DEC_BATCH, n_pages).astype(jnp.int32)
    return {
        "x_prompt": nrm(ks[1], (BATCH, SEQ, D_MODEL)),
        "x_sample": nrm(ks[2], (DEC_BATCH, DEC_SEQ, D_MODEL)),
        "p_prompt": nrm(ks[3], (DEPTH, BATCH, SEQ, D_PLE)),
        "p_sample": nrm(ks[4], (DEPTH, DEC_BATCH, DEC_SEQ, D_PLE)),
        "cache_k": nrm(ks[5], (DEPTH, n_pool, PAGE_SIZE, H_ATT, 2 * DK_ATT)),
        "cache_v": nrm(ks[6], (DEPTH, n_pool, PAGE_SIZE, H_ATT, DV_ATT)),
        "state_rnn": nrm(ks[7], (DEPTH, DEC_BATCH, H_RNN, DK_RNN, DV_RNN), 0.3),
        "state_ffn_conv": nrm(ks[8], (DEPTH, DEC_BATCH, CONV_W - 1, D_FF)),
        "page_table": page_table,
        "norm_mix": gain(ks[9], (DEPTH, D_MODEL)),
        "w_in": nrm(ks[10], (DEPTH, D_MODEL, D_IN), D_MODEL ** -0.5),
        "q_norm": gain(ks[11], (DEPTH, DK_ATT)),
        "k_norm": gain(ks[12], (DEPTH, DK_ATT)),
        "lam_q1": nrm(ks[13], (DEPTH, DK_ATT), 0.1),
        "lam_k1": nrm(ks[14], (DEPTH, DK_ATT), 0.1),
        "lam_q2": nrm(ks[15], (DEPTH, DK_ATT), 0.1),
        "lam_k2": nrm(ks[16], (DEPTH, DK_ATT), 0.1),
        "att_out_norm": gain(ks[17], (DEPTH, DV_ATT)),
        "rnn_out_norm": gain(ks[18], (DEPTH, DV_RNN)),
        "lower_bounds": nrm(ks[19], (DEPTH + 1, RNN_K_W), 0.1),
        "w_out": nrm(ks[20], (DEPTH, D_MIX, D_MODEL), D_MIX ** -0.5),
        "norm_ffn": gain(ks[21], (DEPTH, D_MODEL)),
        "w_gate": nrm(ks[22], (DEPTH, D_MODEL, D_FF), D_MODEL ** -0.5),
        "w_up": nrm(ks[23], (DEPTH, D_MODEL, D_FF), D_MODEL ** -0.5),
        "conv_w": nrm(ks[24], (DEPTH, CONV_W, D_FF), CONV_W ** -0.5),
        "conv_b": nrm(ks[25], (DEPTH, D_FF), 0.02),
        "w_down": nrm(ks[26], (DEPTH, D_FF, D_MODEL), D_FF ** -0.5),
        "norm_ple": gain(ks[27], (DEPTH, D_MODEL)),
        "w_ple_gate": nrm(ks[28], (DEPTH, D_MODEL, D_MODEL), D_MODEL ** -0.5),
        "w_ple_proj": nrm(ks[29], (DEPTH, D_PLE, D_MODEL), D_PLE ** -0.5),
    }

def reference(x_prompt, x_sample, p_prompt, p_sample, cache_k, cache_v, state_rnn, state_ffn_conv, page_table,
              norm_mix, w_in, q_norm, k_norm, lam_q1, lam_k1, lam_q2, lam_k2, att_out_norm, rnn_out_norm,
              lower_bounds, w_out, norm_ffn, w_gate, w_up, conv_w, conv_b, w_down, norm_ple, w_ple_gate,
              w_ple_proj):
    B, S = x_prompt.shape[0], x_prompt.shape[1]
    DB, T = x_sample.shape[0], x_sample.shape[1]
    n_pages = page_table.shape[1]
    past = n_pages * PAGE_SIZE
    pos_p = jnp.arange(S, dtype=jnp.int32)
    pos_s = past + jnp.arange(T, dtype=jnp.int32)
    lb_all = jnp.cumsum(jax.nn.softmax(lower_bounds.astype(jnp.float32), axis=0), axis=0)

    yp, ys = x_prompt, x_sample
    kp_l, vp_l, sp_l, cp_l, ks_l, vs_l, ss_l, cs_l = [], [], [], [], [], [], [], []
    for i in range(DEPTH):
        wts = (norm_mix[i], w_in[i], q_norm[i], k_norm[i], lam_q1[i], lam_k1[i], lam_q2[i], lam_k2[i],
               att_out_norm[i], rnn_out_norm[i], w_out[i], norm_ffn[i], w_gate[i], w_up[i], conv_w[i],
               conv_b[i], w_down[i], norm_ple[i], w_ple_gate[i], w_ple_proj[i])
        lam_init = 0.8 - 0.6 * math.exp(-0.3 * i)
        s0_p = jnp.zeros((B, H_RNN, DK_RNN, DV_RNN), jnp.float32)
        c0_p = jnp.zeros((B, CONV_W - 1, D_FF), x_prompt.dtype)
        yp, kp, vp, sp, cp = layer_forward(yp, p_prompt[i], pos_p, attend_prompt, s0_p, c0_p,
                                           lam_init, lb_all[i], wts)
        kp_l.append(kp.reshape(B, S // PAGE_SIZE, PAGE_SIZE, H_ATT, 2 * DK_ATT))
        vp_l.append(vp.reshape(B, S // PAGE_SIZE, PAGE_SIZE, H_ATT, DV_ATT))
        sp_l.append(sp.astype(state_rnn.dtype))
        cp_l.append(cp)
        k_past = cache_k[i, page_table].reshape(DB, past, H_ATT, 2, DK_ATT)
        v_past = cache_v[i, page_table].reshape(DB, past, H_ATT, DV_ATT)
        attend_s = functools.partial(attend_sample, k_past=k_past, v_past=v_past)
        ys, ks_, vs_, ss_, cs_ = layer_forward(ys, p_sample[i], pos_s, attend_s, state_rnn[i], state_ffn_conv[i],
                                               lam_init, lb_all[i], wts)
        ks_l.append(ks_)
        vs_l.append(vs_)
        ss_l.append(ss_.astype(state_rnn.dtype))
        cs_l.append(cs_)

    k_prompt = jnp.stack(kp_l)
    v_prompt = jnp.stack(vp_l)
    rnn_prompt = jnp.stack(sp_l)
    conv_prompt = jnp.stack(cp_l)
    k_sample = jnp.stack(ks_l)
    v_sample = jnp.stack(vs_l)
    rnn_sample = jnp.stack(ss_l)
    conv_sample = jnp.stack(cs_l)
    return (yp, ys, k_prompt, v_prompt, rnn_prompt, conv_prompt, k_sample, v_sample, rnn_sample, conv_sample)


_drawn_inputs = setup_inputs


def setup_inputs(seed=0):
    import zlib

    import numpy as np

    out = dict(_drawn_inputs(seed))
    spreads = {}
    factors = {'q_norm': 5.816,
     'k_norm': 3.131,
     'lam_k1': 3.233,
     'lam_k2': 2.911,
     'att_out_norm': 6.01,
     'rnn_out_norm': 8.0,
     'norm_ffn': 2.819,
     'conv_b': 6.787,
     'norm_ple': 8.0}
    for name, (base, spread) in spreads.items():
        noise = np.random.default_rng([zlib.crc32(name.encode()), seed]).standard_normal(out[name].shape)
        drawn = base * np.exp(spread * noise) if base else spread * noise
        out[name] = __import__('jax').numpy.asarray(drawn.astype(out[name].dtype))
    for name, factor in factors.items():
        out[name] = (out[name] * factor).astype(out[name].dtype)
    return out
```

```python
from contextlib import ExitStack

import numpy as np

import concourse.bass as bass
from concourse import mybir

F32 = mybir.dt.float32
F32R = mybir.dt.float32r
I32 = mybir.dt.int32
ALU = mybir.AluOpType
ACT = mybir.ActivationFunctionType
AX = mybir.AxisListType

P = 128
D = 2048
SEQ = 512
NS = 8
T = SEQ + NS
TH = T // 2
KT = D // P
HEADS = 8
DK = 64
PAGE = 128
PAGES = 2
NPG = NS * PAGES
PAST = PAGE * PAGES
D_FF = 5632
FB = D_FF // P
GROUPS = 4
GF = FB // GROUPS
PLE = 256
CHUNK = 16
NCH = SEQ // CHUNK
CPB = P // CHUNK
EPS = 1e-6
LAM_INIT = 0.8 - 0.6
SCALE = DK ** -0.5
KC = 8
DOWN_TILES = (6, 5)
GATE_TILES = 6

BLOCK_AT = {"q": 0, "k": 1024, "v": 2048, "f": 4096, "i": 5120, "r": 3072, "g": 6144}
BLOCKS = list(BLOCK_AT)

HEAD_CHUNKS = 2 * len(BLOCKS)
OUT_CHUNKS = 2 * KT
FF_CHUNKS = 4 * GF
DOWN_CHUNKS = 2 * KT
GROUP_CHUNKS = FF_CHUNKS + DOWN_CHUNKS
PLE_CHUNKS = 3 * KT
C_OUT = HEADS * HEAD_CHUNKS
C_FFN = C_OUT + OUT_CHUNKS
C_PLE = C_FFN + GROUPS * GROUP_CHUNKS
C_END = C_PLE + PLE_CHUNKS

ATTENTION = {
    5: ["ssq_q"], 7: ["rot_q"], 9: ["ssq_k"], 11: ["rot_k"],
    12: ["pages0"], 13: ["pages1"], 14: ["v_nat", "k_nat"], 15: ["score0"],
    16: ["s_score"], 17: ["score1"], 18: ["s_prob", "w0"], 19: ["score2"], 20: ["w1"],
    21: ["score3"], 22: ["w2"], 24: ["w3", "s_out"], 25: ["s_turn", "att_out"], 27: ["ssq_a"],
}
RECURRENCE = {
    1: ["i_nat"], 4: ["kh_nat"], 5: ["intra"], 6: ["upd0"], 8: ["upd1", "rnn0"], 10: ["upd2", "rnn1"],
    12: ["upd3", "rnn2"], 15: ["rnn3"], 16: ["s_upd"], 18: ["s_rnn"], 20: ["ssq_r"],
}
HALVES = 2 * HEAD_CHUNKS


def tasks_of(attention, recurrence):
    plan = []
    for s in range(HALVES):
        plan.append((RECURRENCE.get(s, []) if recurrence else []) + (ATTENTION.get(s, []) if attention else []))
    return plan


class Scratch:

    def __init__(self):
        self.base = [0, 0]

    def place(self, names):
        names = list(names) + (["pad"] if len(names) % 2 else [])
        self.at = {n: (i % 2, i // 2) for i, n in enumerate(names)}
        self.per = len(names) // 2
        self.start = list(self.base)
        self.padded = names[-1] == "pad"

    def close(self, times):
        self.base = [b + times * self.per for b in self.start]

    def place_ffn(self):
        self.at = {"c_old": (0, 0), "c_new": (1, 0)}
        self.per = 1
        self.start = list(self.base)
        self.padded = False

    def close_ffn(self):
        self.base = [self.start[0] + GROUPS, self.start[1] + FB]

    def task(self, name, it=0):
        b, i = self.at[name]
        return b, it * self.per + (self.start[b] + i + 1)


ROWS_A = {"norm_mix": 0, "norm_ffn": 16, "norm_ple": 32, "lb0": 48, "lb1": 56, "q": 64, "k": 65, "att": 66, "rnn": 67}
NROWS_A = 68
COL_CW = [NROWS_A, NROWS_A + FB, NROWS_A + 2 * FB, NROWS_A + 3 * FB]
NCOLS = NROWS_A + 4 * FB
FF_STEPS = 4

_K = {}
_n = 0
for _name, _w in (("ident", P), ("ones", P), ("eps", 1),
                  ("swap", P), ("ones64", P), ("cos", T), ("sin", T),
                  ("causal", SEQ), ("restart", SEQ), ("chunk_pairs", P), ("chunk_of", CPB),
                  ("pad_q", NS * 16), ("delta8", NS * NS), ("delta_p", NS), ("pairs", NS),
                  ("coef", 2), ("maps", 2)):
    _K[_name] = (_n, _w)
    _n += _w
NCONST = _n
NKEPT = _K["swap"][0]


def constants():
    c = np.zeros((P, NCONST), np.float32)

    def put(name, a):
        at, w = _K[name]
        c[: a.shape[0], at:at + w] = a

    p = np.arange(P)
    put("ident", np.eye(P, dtype=np.float32))
    swap = np.zeros((P, P), np.float32)
    for d in range(P):
        if d % DK < DK // 2:
            swap[d + DK // 2, d] = -1.0
        else:
            swap[d - DK // 2, d] = 1.0
    put("swap", swap)
    put("ones64", (p[:, None] // DK == p[None, :] // DK).astype(np.float32))
    put("ones", np.ones((P, P), np.float32))
    half = DK // 2
    inv = (np.float32(1.0) / np.power(np.float32(10000.0), np.arange(half, dtype=np.float32) * np.float32(2.0 / DK))).astype(np.float32)
    pos = np.concatenate([np.arange(SEQ), np.full(NS, PAST)]).astype(np.float32)
    ang = (inv[p % half][:, None] * pos[None, :]).astype(np.float32)
    put("cos", np.cos(ang).astype(np.float32))
    put("sin", np.sin(ang).astype(np.float32))
    causal = np.zeros((P, SEQ), np.float32)
    causal[:, SEQ - P:] = np.where(p[None, :] <= p[:, None], 0.0, -1e30)
    put("causal", causal)
    put("restart", np.tile((np.arange(SEQ) % CHUNK != 0).astype(np.float32), (P, 1)))
    same = p[:, None] // CHUNK == p[None, :] // CHUNK
    put("chunk_pairs", (same & (p[:, None] <= p[None, :])).astype(np.float32))
    put("chunk_of", (p[:, None] // CHUNK == np.arange(CPB)[None, :]).astype(np.float32))
    pad = np.zeros((P, NS, NS, 2), np.float32)
    for b in range(NS):
        for m in range(2):
            pad[m * DK:(m + 1) * DK, b, b, m] = 1.0
    put("pad_q", pad.reshape(P, -1))
    put("delta8", np.tile(np.eye(NS, dtype=np.float32).reshape(1, -1), (P, 1)))
    put("delta_p", np.eye(NS, dtype=np.float32))
    put("pairs", (np.arange(16)[:, None] // 2 == np.arange(NS)[None, :]).astype(np.float32))
    put("coef", np.stack([np.arange(16) % 2 == 0, -(np.arange(16) % 2.0)], 1).astype(np.float32))
    put("eps", np.full((P, 1), EPS, np.float32))
    put("maps", np.stack([p < DK, p >= DK], 1).astype(np.float32))
    return c


def program(nc, a, o):
    ctx = ExitStack()
    early, heads, late = ExitStack(), ExitStack(), ExitStack()

    def sem(name):
        return ctx.enter_context(nc.semaphore(name))

    def sb(name, shape, dt=F32, into=ctx):
        return into.enter_context(nc.sbuf_tensor(name, shape, dt))

    mix_d = nc.dram_tensor("mix_scratch", [KT, P, T], F32, kind="Internal").ap()
    xt_d = nc.dram_tensor("x_scratch", [KT, P, T], F32, kind="Internal").ap()

    const = sb("const", [P, NKEPT])
    vecs = sb("vecs", [P, NCOLS])
    act_hi = sb("act_hi", [P, KT, T], F32R)
    act_lo = sb("act_lo", [P, KT, T], F32R)
    w_raw = sb("w_raw", [P, 2, KC, P])
    w_hi = sb("w_hi", [P, 2, KC, P], F32R)
    w_lo = sb("w_lo", [P, 2, KC, P], F32R)
    R = sb("R", [P, T])
    sq_sum = sb("sq_sum", [P, T])
    sqx = sb("sqx", [P, 2, T])
    pad_out = sb("pad_out", [32, 1])

    def K(name):
        at, w = _K[name]
        return const[:, at:at + w] if at < NKEPT else tables[:, at - NKEPT:at - NKEPT + w]

    def vec(row, n=1):
        return vecs[:, row:row + n]

    ident = K("ident")

    x_nat = sb("x_nat", [P, 2, D], into=early)
    xT0 = sb("xT0", [P, KT, T], into=early)
    rows_a = sb("rows_a", [P, P], into=early)
    rows_b = sb("rows_b", [P, 2, P], into=early)
    early.close()

    def hb(name, shape, dt=F32):
        return sb(name, shape, dt, heads)

    tables = hb("tables", [P, NCONST - NKEPT])
    lamv = hb("lamv", [P, 4, DK])
    lams = hb("lams", [P, 8])
    lam = hb("lam", [P, 1])
    coef = hb("coef", [16, 1])
    lb = hb("lb", [P, HEADS])
    oml = hb("oml", [P, HEADS])
    lbt = hb("lbt", [P, 3, HEADS])
    gain_a = hb("gain_a", [P, 1])
    pages_sb = hb("pages_sb", [1, NPG], I32)
    z_q = hb("z_q", [P, T])
    z_k = hb("z_k", [P, T])
    z_v = hb("z_v", [P, T])
    sq, rot, zn = sqx[:, 0, :], sqx[:, 1, :], sq_sum
    rr = hb("rr", [P, T])
    q_rot, k_rot = z_q, z_k
    q_map = hb("q_map", [P, 2, SEQ])
    k_nat = hb("k_nat", [P, 5, P])
    v_nat = hb("v_nat", [P, 5, P])
    score = hb("score", [P, 2, SEQ])
    wgt = hb("wgt", [P, SEQ])
    wT = hb("wT", [P, 10, P])
    row_max = hb("row_max", [P, 2])
    neg_max = hb("neg_max", [P, 2])
    row_sum = hb("row_sum", [P, 2])
    row_inv = hb("row_inv", [P, 2])
    row_lam = hb("row_lam", [P, 1])
    k_pages = hb("k_pages", [P, NPG, P])
    v_pages = k_pages
    kT = hb("kT", [P, NS, PAST + 1])
    q_pad = hb("q_pad", [P, NS, 16])
    s_p = hb("s_p", [16, PAST + 1])
    s_stat = hb("s_stat", [16, 5])
    w_sum = hb("w_sum", [P, NPG])
    w_pad = hb("w_pad", [P, NPG, NS])
    v_two = hb("v_two", [P, 16])
    new_w = hb("new_w", [P, NS])
    new_v = hb("new_v", [P, P])
    s_o = hb("s_o", [NS, P])
    oT = hb("oT", [P, T])
    mix_a = hb("mix_a", [P, T])
    mix_r = hb("mix_r", [P, T])
    r_o = hb("r_o", [P, T])
    r_g = r_o
    z_f = hb("z_f", [P, T])
    z_i = hb("z_i", [P, T])
    z_r = hb("z_r", [P, T])
    z_g = hb("z_g", [P, T])
    r_k = hb("r_k", [P, T])
    f_s = hb("f_s", [P, NS])
    r_b = hb("r_b", [P, SEQ])
    r_e = hb("r_e", [P, SEQ])
    r_kd = r_b
    r_kh = hb("r_kh", [P, SEQ])
    r_qd = z_r[:, 0:SEQ]
    i_nat = hb("i_nat", [P, 5, P])
    ks_nat = hb("ks_nat", [NS, P])
    kh_nat = hb("kh_nat", [P, 4, P])
    intra = hb("intra", [P, 4, P])
    state = hb("state", [P, 2, CPB, P])
    s_state = hb("s_state", [P, NS, P])
    v_chunks = hb("v_chunks", [P, CPB, P])
    s_iexp = v_chunks[0:NS]
    heads.close()

    def lt(name, shape, dt=F32):
        return sb(name, shape, dt, late)

    xT = lt("xT", [P, KT, T])
    pT_hi = lt("pT_hi", [P, 2, T], F32R)
    pT_lo = lt("pT_lo", [P, 2, T], F32R)
    out_, ffn_, ple_ = ExitStack(), ExitStack(), ExitStack()
    p_nat = sb("p_nat", [P, 5, PLE], into=out_)
    pT = sb("pT", [P, 2, T], into=out_)
    out_.close()
    u_hi = sb("u_hi", [P, GF, T], F32R, ffn_)
    u_lo = sb("u_lo", [P, GF, T], F32R, ffn_)
    ffg = sb("ffg", [P, T + 2], into=ffn_)
    ffc = sb("ffc", [P, T], into=ffn_)
    ffs = sb("ffs", [P, T], into=ffn_)
    ffu = sb("ffu", [P, T], into=ffn_)
    conv_in = sb("conv_in", [16, GF * P], into=ffn_)
    conv_old = sb("conv_old", [P, GF, NS, 2], into=ffn_)
    conv_new = conv_in[0:10]
    ffn_.close()
    gate = sb("gate", [P, T], into=ple_)
    y_t = sb("y_t", [P, 2, T], into=ple_)
    y_nat = sb("y_nat", [P, 2, 5, P], into=ple_)
    ple_.close()
    late.close()

    G = [ctx.enter_context(nc.psum_tensor(f"product{i}", [P, 2, 512], F32)) for i in range(2)]
    M = [ctx.enter_context(nc.psum_tensor(f"scratch{i}", [P, 2, 512], F32)) for i in range(2)]

    w_landed = [sem(f"w_landed{i}") for i in range(2)]
    w_hi_ready, w_lo_ready, w_used = sem("w_hi_ready"), sem("w_lo_ready"), sem("w_used")
    g_free = [sem(f"product{i}_free") for i in range(2)]
    full = [sem(f"scratch{i}_full") for i in range(2)]
    free = [sem(f"scratch{i}_free") for i in range(2)]
    S = {}

    def flag(name):
        if name not in S:
            S[name] = sem(name)
        return S[name]

    def two(ap):
        return ap.rearrange("p (a b) -> p a b", a=2)

    def flat(ap):
        return ap.rearrange("p a b -> p (a b)")

    def m_wide(b):
        return M[b][:, :, 0:TH]

    scratch = Scratch()
    plans = [tasks_of(True, False), tasks_of(True, True), tasks_of(False, True)]
    spans = [(0, 1), (1, HEADS), (HEADS, HEADS + 1)]

    PER_HEAD = [4, 3]
    g_out = [HEADS * 4, HEADS * 3]
    g_ffn = [x + KT // 2 for x in g_out]
    g_per_group = GF + KT // 2
    g_ple = [x + GROUPS * g_per_group for x in g_ffn]

    early_names = [f"x{t}{i}" for t in range(4) for i in range(2)] + ["xs", "rows_a", "rows_b", "ssx"]

    def phases(visit):
        scratch.base = [0, 0]
        scratch.place(early_names)
        visit("early", None)
        scratch.close(1)
        for plan, (h0, h1) in zip(plans, spans):
            names = [n for slot in plan for n in slot]
            scratch.place(names)
            visit("heads", (plan, h0, h1))
            scratch.close(h1 - h0)
        scratch.place(["p_turn", "ps_turn", "ss_out"])
        visit("out", None)
        scratch.close(1)
        scratch.place_ffn()
        visit("ffn", None)
        scratch.close_ffn()
        scratch.place(["ss_ffn"])
        visit("mid", None)
        scratch.close(1)
        scratch.place(["pp0", "y0", "pp1", "y1"])
        visit("ple", None)
        scratch.close(KT // 2)

    def evacuated(name, h):
        blk = BLOCKS.index(name)
        g = blk % 2
        return g_free[g], h * PER_HEAD[g] + (blk // 2 + 1)

    def read(name, it):
        b, v = scratch.task(name, it)
        return free[b], v

    block = ctx.enter_context(nc.Block())

    @block.sync
    def _(sp):
        w_in = a["w_in"][0].rearrange("(k p) m -> p k m", p=P)
        w_out = a["w_out"][0].rearrange("(k p) m -> p k m", p=P)
        w_gate = a["w_gate"][0].rearrange("(k p) m -> p k m", p=P)
        w_up = a["w_up"][0].rearrange("(k p) m -> p k m", p=P)
        w_down = a["w_down"][0].rearrange("(k p) m -> p k m", p=P)
        w_pg = a["w_ple_gate"][0].rearrange("(k p) m -> p k m", p=P)
        w_pp = a["w_ple_proj"][0].rearrange("(k p) m -> p k m", p=P)

        def load(c, slot, w, k0, n, col):
            src = w[:, bass.ds(k0, n), bass.ds(col, P)]
            if not isinstance(c, int) or c >= 2:
                sp.wait_ge(w_hi_ready, c - 1)
                sp.wait_ge(w_lo_ready, c - 1)
            sp.dma_start(w_raw[:, slot, 0:n, :], src).then_inc(w_landed[slot], 16)

        def setup():
            sp.dma_start(const[:, :], a["consts"][:, 0:NKEPT]).then_inc(flag("const_in"), 16)
            rows = [("norm_mix", 0, 16), ("norm_ffn", 16, 16), ("norm_ple", 32, 16)]
            for name, r, n in rows:
                sp.dma_start(rows_a[r:r + n, :], a[name][0].rearrange("(b p) -> b p", p=P)).then_inc(flag("rows_in"), 16)
            sp.dma_start(rows_a[48:64, :], a["lower_bounds"].rearrange("r (b p) -> (r b) p", p=P)).then_inc(flag("rows_in"), 16)
            for name, r in (("q_norm", 64), ("k_norm", 65)):
                for m in range(2):
                    sp.dma_start(rows_a[r:r + 1, m * DK:(m + 1) * DK], a[name]).then_inc(flag("rows_in"), 16)
            for name, r in (("att_out_norm", 66), ("rnn_out_norm", 67)):
                sp.dma_start(rows_a[r:r + 1, :], a[name]).then_inc(flag("rows_in"), 16)
            for j in range(4):
                src = a["conv_w"][0, j] if j < 3 else a["conv_b"][0]
                sp.dma_start(rows_b[(j % 2) * FB:(j % 2 + 1) * FB, j // 2, :], src.rearrange("(b p) -> b p", p=P)).then_inc(flag("rows_in"), 16)
            for t in range(5):
                if t >= 2:
                    b, v = scratch.task(f"x{t - 2}1")
                    sp.wait_ge(full[b], v)
                if t < 4:
                    sp.dma_start(x_nat[:, t % 2, :], a["x_prompt"][0, t * P:(t + 1) * P, :]).then_inc(flag(f"x_in{t}"), 16)
                else:
                    sp.dma_start(x_nat[0:NS, 0, :], a["x_sample"].rearrange("b t d -> (b t) d")).then_inc(flag(f"x_in{t}"), 16)
            load(0, 0, w_in, 0, KC, BLOCK_AT["q"])
            load(1, 1, w_in, KC, KC, BLOCK_AT["q"])
            sp.wait_ge(flag("xT_written"), 16)
            sp.wait_ge(flag("act_lo_ready"), KT)
            sp.wait_ge(flag("sq_sum_done"), KT)
            sp.dma_start(tables[:, :], a["consts"][:, NKEPT:]).then_inc(flag("tables_in"), 16)
            for n, name in enumerate(("lam_q1", "lam_k1", "lam_q2", "lam_k2")):
                sp.dma_start(lamv[:, n, :], a[name].to_broadcast([P, DK])).then_inc(flag("lam_in"), 16)
            sp.dma_start(pages_sb[:, :], a["page_table"].rearrange("b n -> (b n)").rearrange("(o n) -> o n", o=1)).then_inc(flag("pages_in"), 16)
            sp.wait_ge(flag("pages_in"), 16)

        def weights(h, s):
            if s % 2 == 0:
                j = s // 2
                name = BLOCKS[j // 2]
                load(h * HEAD_CHUNKS + j, j % 2, w_in, (j % 2) * KC, KC, h * P + BLOCK_AT[name])

        def step(plan, it, h, r, pages):
            attention = any("ssq_q" in x for x in plan)
            recurrence = any("ssq_r" in x for x in plan)
            for s in range(HALVES):
                if attention and (not isinstance(h, int) or s >= 4):
                    weights(h, s)
                if attention and s == 4:
                    if not isinstance(h, int):
                        sp.wait_ge(flag("mix_a_done"), h)
                    for n in range(NPG):
                        sp.dma_start(k_pages[:, n, :], a["cache_k"][0, bass.ds(pages[n], 1), :, bass.ds(h, 1), :].rearrange("g t h d -> (g t) (h d)")).then_inc(flag("k_pages_in"), 16)
                if attention and s == 18:
                    for x in ("pages0", "pages1"):
                        b, v = scratch.task(x, it)
                        sp.wait_ge(full[b], v)
                    for n in range(NPG):
                        sp.dma_start(v_pages[:, n, :], a["cache_v"][0, bass.ds(pages[n], 1), :, bass.ds(h, 1), :].rearrange("g t h d -> (g t) (h d)")).then_inc(flag("v_pages_in"), 16)
                if recurrence and s == 4:
                    if not attention:
                        sp.wait_ge(flag("mix_a_done"), HEADS)
                    sp.dma_start(s_state[:, :, :], a["state_rnn"][0, :, bass.ds(r, 1), :, :].rearrange("b h k v -> k (b h) v")).then_inc(flag("s_state_in"), 16)

        pages = []

        def visit(what, arg):
            if what == "early":
                setup()
                for n in range(NPG):
                    pages.append(sp.value_load(pages_sb[0:1, n:n + 1], min_val=0, max_val=a["cache_k"].shape[1] - 1))
            elif what == "heads":
                plan, h0, h1 = arg
                if h0 == 0:
                    step(plan, 0, 0, None, pages)
                elif h1 == HEADS:
                    with sp.Fori(h0, h1) as h:
                        step(plan, h - 1, h, h - 1, pages)
                else:
                    load(C_OUT, 0, w_out, 0, KC, 0)
                    load(C_OUT + 1, 1, w_out, KC, KC, 0)
                    step(plan, 0, HEADS, HEADS - 1, pages)
            elif what == "out":
                sp.wait_ge(flag("mix_a_out"), HEADS * 16)
                sp.wait_ge(flag("mix_r_out"), HEADS * 16)
                sp.wait_ge(flag("k_nat_out"), HEADS * 32)
                sp.wait_ge(flag("v_nat_out"), HEADS * 32)
                sp.wait_ge(flag("s_state_out"), HEADS * 16)
                sp.wait_ge(flag("state_out"), HEADS * 16)
                for k in range(KT):
                    sp.dma_start(xT[:, k, :], mix_d[k]).then_inc(flag(f"mix_in{k}"), 16)
                sp.dma_start(o["conv_sample"][0, :, 0, :], a["state_ffn_conv"][0, :, 1, :]).then_inc(flag("conv_out"), 16)
                for j in range(4):
                    sp.dma_start(p_nat[:, j, :], a["p_prompt"][0, 0, j * P:(j + 1) * P, :]).then_inc(flag("p_in"), 16)
                sp.dma_start(p_nat[0:NS, 4, :], a["p_sample"][0, :, 0, :]).then_inc(flag("p_in"), 16)
                for k in range(KT):
                    sp.wait_ge(flag("act_lo_ready"), KT + k + 1)
                    sp.dma_start(xT[:, k, :], xt_d[k]).then_inc(flag("x_back"), 16)
                load(C_OUT + 2, 0, w_out, 0, KC, P)
                load(C_OUT + 3, 1, w_out, KC, KC, P)
                with sp.Fori(1, KT // 2) as it:
                    for j in range(4):
                        load(it * 4 + (C_OUT + j), j % 2, w_out, (j % 2) * KC, KC, it * (2 * P) + (j // 2) * P)
            elif what == "ffn":
                with sp.Fori(0, GROUPS) as g:
                    def ffn_chunk(f, j):
                        w = w_gate if j < 2 else w_up
                        load(g * GROUP_CHUNKS + f * 4 + (C_FFN + j), j % 2, w, (j % 2) * KC, KC, g * (GF * P) + f * P)

                    ffn_chunk(0, 0)
                    ffn_chunk(0, 1)
                    sp.wait_ge(full[0], scratch.task("c_old", g)[1] - 1)
                    sp.wait_ge(flag("conv_out"), g * 32 + 16)
                    sp.dma_start(conv_in[:, :], a["state_ffn_conv"][0].rearrange("b w f -> (b w) f")[:, bass.ds(g * (GF * P), GF * P)]).then_inc(flag("conv_in"), 16)
                    ffn_chunk(0, 2)
                    ffn_chunk(0, 3)
                    with sp.Fori(1, GF) as f:
                        for j in range(4):
                            ffn_chunk(f, j)
                    with sp.Fori(0, KT // 2) as m:
                        for j in range(4):
                            k0, n = ((0, 6), (6, 5))[j % 2]
                            load(g * GROUP_CHUNKS + m * 4 + (C_FFN + FF_CHUNKS + j), j % 2, w_down, g * GF + k0, n, m * (2 * P) + (j // 2) * P)
            elif what == "ple":
                with sp.Fori(0, KT // 2) as m:
                    for j in range(6):
                        c, col = m * 6 + (C_PLE + j), m * (2 * P) + (j // 3) * P
                        if j % 3 < 2:
                            load(c, j % 2, w_pg, (j % 3) * GATE_TILES, GATE_TILES, col)
                        else:
                            n = KT - 2 * GATE_TILES
                            load(c, j % 2, w_pg, 2 * GATE_TILES, n, col)
                            sp.dma_start(w_raw[:, j % 2, n:GATE_TILES, :], w_pp[:, :, bass.ds(col, P)]).then_inc(w_landed[j % 2], 16)
                sp.wait_ge(flag("y_out0"), KT * 16)
                sp.wait_ge(flag("y_out1"), KT * 16)
                sp.wait_ge(flag("conv_out"), 16 + GROUPS * 2 * 16)

        phases(visit)

    @block.tensor
    def _(pe):
        def split_ready(c):
            pe.wait_ge(w_lo_ready, c + 1)

        def product_free(g, n):
            if not isinstance(n, int) or n > 0:
                pe.wait_ge(g_free[g], n)

        def task(name, it, waits=(), counts=(), reads=()):
            b, v = scratch.task(name, it)
            if not isinstance(v, int) or v >= 2:
                pe.wait_ge(free[b], v - 1)
            others = [scratch.at[x][1] for x in reads if scratch.at[x][0] != b]
            if others:
                last = [x for x in reads if scratch.at[x] == (1 - b, max(others))][0]
                pe.wait_ge(*read(last, it))
            for f, n in waits:
                pe.wait_ge(flag(f), n)
            for sem_, n in counts:
                pe.wait_ge(sem_, n)
            return b

        def turn(out, in_, n):
            if n <= 32:
                return pe.matmul(out, in_, ident[0:n, 0:n], start=True, stop=True)
            return pe.transpose(out, in_, ident[0:n, 0:n])

        def wide(name, it, waits, lhsT, rhs):
            wide_into(task(name, it, waits), lhsT, rhs)

        def wide_into(b, lhsT, rhs):
            for half in range(2):
                mm = pe.matmul(M[b][:, half, 0:TH], lhsT, rhs[:, half * TH:(half + 1) * TH], start=True, stop=True)
            mm.then_inc(full[b], 1)

        def small(name, it, h, r):
            n = None if h is None else h + 1
            m = None if r is None else r + 1
            if name == "ssq_q":
                wide(name, it, [("sq_q", n)], K("ones64"), sq)
            elif name == "rot_q":
                wide(name, it, [("zn_done", h * 2 + 1)], K("swap"), zn)
            elif name == "ssq_k":
                wide(name, it, [("sq_k", n)], K("ones64"), sq)
            elif name == "rot_k":
                wide(name, it, [("zn_done", h * 2 + 2)], K("swap"), zn)
            elif name in ("pages0", "pages1"):
                i = int(name[-1])
                b = task(name, it, [("k_pages_in", h * (NPG * 16) + NPG * 16)])
                for y in range(8):
                    mm = turn(M[b][:, y // 4, (y % 4) * P:(y % 4 + 1) * P], k_pages[:, i * 8 + y, :], P)
                mm.then_inc(full[b], 1)
            elif name in ("v_nat", "k_nat", "i_nat"):
                if name == "v_nat":
                    b = task(name, it, [], [evacuated("v", h)])
                    src = z_v
                elif name == "k_nat":
                    b = task(name, it, [("k_rot_done", n)])
                    src = k_rot
                else:
                    b = task(name, it, [("r_k_done", m)], [evacuated("i", r)])
                    src = z_i
                for j in range(4):
                    turn(M[b][:, 0, j * P:(j + 1) * P], src[:, j * P:(j + 1) * P], P)
                mm = turn(M[b][0:NS, 1, 0:P], src[:, SEQ:T], P)
                if name == "i_nat":
                    mm = turn(M[b][0:NS, 1, P:2 * P], r_k[:, SEQ:T], P)
                mm.then_inc(full[b], 1)
            elif name.startswith("score"):
                i = int(name[-1])
                w = (i + 1) * P
                b = task(name, it, [("q_map_done", n), ("k_rot_done", n)])
                for m_ in range(2):
                    mm = pe.matmul(M[b][:, m_, 0:w], q_map[:, m_, i * P:(i + 1) * P], k_rot[:, 0:w], start=True, stop=True)
                mm.then_inc(full[b], 1)
            elif name == "s_score":
                b = task(name, it, [("q_pad_done", n), ("kT_new_done", n)], (), ["pages0", "pages1"])
                for y in range(NS):
                    mm = pe.matmul(M[b][0:16, 0, 0:PAST + 1], q_pad[:, y, :], kT[:, y, :], start=y == 0, stop=y == NS - 1)
                mm.then_inc(full[b], 1)
            elif name in ("w0", "w1", "w2", "w3"):
                i = int(name[-1])
                b = task(name, it, [("wgt_done", h * 4 + (i + 1))])
                for j in range(i + 1):
                    mm = turn(M[b][:, 0, j * P:(j + 1) * P], wgt[:, j * P:(j + 1) * P], P)
                mm.then_inc(full[b], 1)
            elif name == "s_prob":
                b = task(name, it, [("s_p_done", n), ("v_two_done", n)])
                for y in range(2):
                    turn(M[b][:, 0, y * 16:(y + 1) * 16], s_p[:, y * P:(y + 1) * P], 16)
                turn(M[b][0:16, 1, 0:P], v_two[:, :], P).then_inc(full[b], 1)
            elif name == "s_out":
                b = task(name, it, [("w_pad_done", n), ("new_w_done", n), ("v_pages_in", h * (NPG * 16) + NPG * 16)])
                out = M[b][0:NS, 0, 0:P]
                for y in range(NPG):
                    pe.matmul(out, w_pad[:, y, :], v_pages[:, y, :], start=y == 0, stop=False)
                pe.matmul(out, new_w[:, :], new_v[:, :], start=False, stop=True).then_inc(full[b], 1)
            elif name == "s_turn":
                b = task(name, it, [], (), ["s_out"])
                turn(M[b][:, 0, 0:NS], s_o[:, :], NS).then_inc(full[b], 1)
            elif name == "att_out":
                b = task(name, it, [], (), ["w2", "w3", "v_nat"])
                for i in range(4):
                    for j in range(i + 1):
                        mm = pe.matmul(M[b][:, 0, i * P:(i + 1) * P], v_nat[:, j, :], wT[:, i * (i + 1) // 2 + j, :], start=j == 0, stop=j == i)
                mm.then_inc(full[b], 1)
            elif name == "ssq_a":
                wide(name, it, [("sq_a", n)], K("ones"), sq)
            elif name == "kh_nat":
                b = task(name, it, [("r_kh_done", m)])
                for j in range(4):
                    mm = turn(M[b][:, 0, j * P:(j + 1) * P], r_kh[:, j * P:(j + 1) * P], P)
                mm.then_inc(full[b], 1)
            elif name == "intra":
                b = task(name, it, [("r_kd_done", m), ("r_qd_done", m)])
                for j in range(4):
                    t = slice(j * P, (j + 1) * P)
                    mm = pe.matmul(M[b][:, 0, t], r_kd[:, t], r_qd[:, t], start=True, stop=True)
                mm.then_inc(full[b], 1)
            elif name.startswith("upd"):
                j = int(name[-1])
                b = task(name, it, [("v_chunks_done", r * 4 + (j + 1))], (), ["kh_nat"])
                for y in range(2):
                    mm = pe.matmul(M[b][:, y, :], kh_nat[:, j, :], flat(v_chunks[:, y * 4:(y + 1) * 4, :]), start=True, stop=True)
                mm.then_inc(full[b], 1)
            elif name in ("rnn0", "rnn1", "rnn2", "rnn3"):
                j = int(name[-1])
                b = task(name, it, [("state_done", r * 28 + (j * 7 + 7))], (), ["intra"])
                mm = pe.matmul(M[b][:, 0, 0:P], i_nat[:, j, :], intra[:, j, :], start=True, stop=False, skip_group_check=True)
                for c in range(CPB):
                    if j == 0 and c == 0:
                        continue
                    mm = pe.matmul(M[b][:, 0, c * CHUNK:(c + 1) * CHUNK], state[:, j % 2, c, :], r_qd[:, (j * CPB + c) * CHUNK:(j * CPB + c + 1) * CHUNK],
                                   start=False, stop=c == CPB - 1, skip_group_check=True)
                mm.then_inc(full[b], 1)
            elif name == "s_upd":
                b = task(name, it, [("s_iexp_done", m)], (), ["i_nat"])
                for y in range(2):
                    mm = pe.matmul(M[b][:, y, :], ks_nat[:, :], flat(s_iexp[:, y * 4:(y + 1) * 4, :]), start=True, stop=True)
                mm.then_inc(full[b], 1)
            elif name == "s_rnn":
                b = task(name, it, [], (), ["s_upd"])
                for y in range(NS):
                    mm = pe.matmul(M[b][:, 0, y:y + 1], s_state[:, y, :], z_r[:, SEQ + y:SEQ + y + 1], start=True, stop=True)
                mm.then_inc(full[b], 1)
            elif name == "ssq_r":
                wide(name, it, [("sq_r", m)], K("ones"), mix_r)

        def pad(it):
            if scratch.padded:
                b = task("pad", it)
                pe.matmul(M[b][0:32, 0, 0:64], ident[:, 0:32], ident[:, 0:64], start=True, stop=True).then_inc(full[b], 1)

        def step(plan, it, h, r):
            for s in range(HALVES):
                if h is not None:
                    j = s // 2
                    c = h * HEAD_CHUNKS + j
                    blk, g = j // 2, (j // 2) % 2
                    if s % 2 == 0:
                        split_ready(c)
                    if s % 4 == 0:
                        product_free(g, h * PER_HEAD[g] + blk // 2)
                    mm = part(g, j % 2, (s % 2) * 4, (s % 4) * 4, 4, s % 4 == 0, s % 4 == 3, act_hi, act_lo)
                    if s % 2 == 1:
                        mm.then_inc(w_used, 1)
                for name in plan[s]:
                    small(name, it, h, r)
            pad(it)

        def part(g, slot, j0, k0, n, first, last, hi, lo, wait_k=None):
            return passes(G[g], slot, j0, k0, n, first, last, hi, lo, wait_k)

        def passes(out, slot, j0, k0, n, first, last, hi, lo, wait_k=None):
            mm = None
            for j in range(n):
                if wait_k is not None:
                    pe.wait_ge(flag(wait_k[0]), wait_k[1] + j)
                for which, (w, x) in enumerate(((w_hi, hi), (w_hi, lo), (w_lo, hi))):
                    for half in range(2):
                        t = slice(half * TH, (half + 1) * TH)
                        mm = pe.matmul(out[:, half, 0:TH], w[:, slot, j0 + j, :], x[:, k0 + j, t],
                                       start=first and j == 0 and which == 0,
                                       stop=last and j == n - 1 and which == 2)
            return mm

        def full_product(g, n_free, c, sizes, hi, lo, wait_k=None):
            product_free(g, n_free)
            k = 0
            for j, n in enumerate(sizes):
                split_ready(c + j)
                slot = j % 2
                mm = part(g, slot, 0, k, n, j == 0, j == len(sizes) - 1, hi, lo,
                          None if wait_k is None else (wait_k[0], wait_k[1] + k))
                mm.then_inc(w_used, 1)
                k += n

        sum_task = None

        def visit(what, arg):
            nonlocal sum_task
            if what == "early":
                pe.wait_ge(flag("const_in"), 16)
                for t in range(4):
                    pe.wait_ge(flag(f"x_in{t}"), 16)
                    for i in range(2):
                        b = task(f"x{t}{i}", 0)
                        for y in range(8):
                            mm = turn(M[b][:, y // 4, (y % 4) * P:(y % 4 + 1) * P], x_nat[:, t % 2, (i * 8 + y) * P:(i * 8 + y + 1) * P], P)
                        mm.then_inc(full[b], 1)
                pe.wait_ge(flag("x_in4"), 16)
                b = task("xs", 0)
                for y in range(16):
                    mm = turn(M[b][:, 0, y * NS:(y + 1) * NS], x_nat[0:NS, 0, y * P:(y + 1) * P], NS)
                mm.then_inc(full[b], 1)
                pe.wait_ge(flag("rows_in"), 14 * 16)
                b = task("rows_a", 0)
                turn(M[b][:, 0, 0:NROWS_A], rows_a[0:NROWS_A, :], NROWS_A).then_inc(full[b], 1)
                b = task("rows_b", 0)
                for j in range(2):
                    mm = turn(M[b][:, 0, j * 2 * FB:(j + 1) * 2 * FB], rows_b[0:2 * FB, j, :], 2 * FB)
                mm.then_inc(full[b], 1)
                wide("ssx", 0, [("sq_sum_done", KT)], K("ones"), sq_sum)
                pe.wait_ge(flag("act_lo_ready"), KT)
                pe.wait_ge(flag("tables_in"), 16)
            elif what == "heads":
                plan, h0, h1 = arg
                if h0 == 0:
                    step(plan, 0, 0, None)
                elif h1 == HEADS:
                    with pe.Fori(h0, h1) as h:
                        step(plan, h - 1, h, h - 1)
                else:
                    step(plan, 0, None, HEADS - 1)
            elif what == "out":
                full_product(0, g_out[0], C_OUT, (KC, KC), act_hi, act_lo, ("act_lo_ready", KT + 1))
                b = task("p_turn", 0, [("p_in", 80)])
                for half in range(2):
                    for j in range(4):
                        mm = turn(M[b][:, half, j * P:(j + 1) * P], p_nat[:, j, half * P:(half + 1) * P], P)
                mm.then_inc(full[b], 1)
                b = task("ps_turn", 0)
                for half in range(2):
                    mm = turn(M[b][:, 0, half * NS:(half + 1) * NS], p_nat[0:NS, 4, half * P:(half + 1) * P], NS)
                mm.then_inc(full[b], 1)
                full_product(1, g_out[1], C_OUT + 2, (KC, KC), act_hi, act_lo)
                with pe.Fori(1, KT // 2) as it:
                    for g in range(2):
                        full_product(g, it + g_out[g], it * 4 + (C_OUT + 2 * g), (KC, KC), act_hi, act_lo)
                wide("ss_out", 0, [("sq_sum_done", 2 * KT)], K("ones"), sq_sum)
                pad(0)
            elif what == "ffn":
                with pe.Fori(0, GROUPS) as g:
                    def ff_block(f, first):
                        n = g * GF + f
                        for x in range(2):
                            full_product(x, g * g_per_group + f + g_ffn[x], g * GROUP_CHUNKS + f * 4 + (C_FFN + 2 * x), (KC, KC), act_hi, act_lo,
                                         ("act_lo_ready", 2 * KT + 1) if first and x == 0 else None)
                            if first and x == 0:
                                b = task("c_old", g, [("conv_in", g * 16 + 16)])
                                for i in range(GF):
                                    mm = turn(M[b][:, 0, i * 16:(i + 1) * 16], conv_in[:, i * P:(i + 1) * P], 16)
                                mm.then_inc(full[b], 1)
                        b = task("c_new", n, [], [(g_free[0], g * g_per_group + f + (g_ffn[0] + 1))])
                        turn(M[b][0:10, 0, 0:P], ffg[:, SEQ:SEQ + 10], P).then_inc(full[b], 1)

                    ff_block(0, True)
                    with pe.Fori(1, GF) as f:
                        ff_block(f, False)
                    with pe.Fori(0, KT // 2) as m:
                        pe.wait_ge(flag("u_done"), g * GF + GF)
                        for x in range(2):
                            full_product(x, g * g_per_group + m + (g_ffn[x] + GF), g * GROUP_CHUNKS + m * 4 + (C_FFN + FF_CHUNKS + 2 * x), DOWN_TILES, u_hi, u_lo)
            elif what == "mid":
                sum_task = scratch.task("ss_ffn", 0)
                pad(0)
            elif what == "ple":
                def y_turn(x, m):
                    b = task(f"y{x}", m, [("y_done", m * 2 + (x + 1))])
                    for j in range(4):
                        turn(M[b][:, 0, j * P:(j + 1) * P], y_t[:, x, j * P:(j + 1) * P], P)
                    turn(M[b][0:NS, 1, 0:P], y_t[:, x, SEQ:T], P).then_inc(full[b], 1)

                def ple(m, x, before):
                    n = KT - 2 * GATE_TILES
                    c = m * 6 + (C_PLE + 3 * x)
                    product_free(x, m + g_ple[x])
                    for j in range(3):
                        slot = (3 * x + j) % 2
                        k = j * GATE_TILES
                        split_ready(c + j)
                        if j == 2:
                            b = task(f"pp{x}", m)
                            passes(M[b], slot, n, 0, GATE_TILES - n, True, True, pT_hi, pT_lo).then_inc(full[b], 1)
                        part(x, slot, 0, k, GATE_TILES if j < 2 else n, j == 0, j == 2, act_hi, act_lo,
                             ("act_lo_ready", 3 * KT + 1 + k) if before is None else None).then_inc(w_used, 1)
                        if j == 0 and before is None:
                            b, v = sum_task
                            pe.wait_ge(free[b], v - 1)
                            pe.wait_ge(flag("sq_sum_done"), (2 + GROUPS) * KT)
                            wide_into(b, K("ones"), sq_sum)
                        if j == 0 and before is not None:
                            y_turn(*before)

                ple(0, 0, None)
                ple(0, 1, (0, 0))
                with pe.Fori(1, KT // 2) as m:
                    ple(m, 0, (1, m - 1))
                    ple(m, 1, (0, m))
                y_turn(1, KT // 2 - 1)

        phases(visit)

    CP = (PAST + 1)

    def pages_view(b):
        return M[b][:, :, :].rearrange("p a (y t) -> p (a y) t", y=2)

    def column(tile, k, n=1):
        return tile[:, bass.ds(k, n), :].rearrange("p a b -> p (a b)")

    @block.scalar
    def _(act):
        def split(c, c2, slot, n=KC):
            act.wait_ge(w_landed[slot], c2 * 16 + 16)
            if not isinstance(c, int) or c >= 2:
                act.wait_ge(w_used, c - 1)
            act.activation(w_hi[:, slot, 0:n, :], w_raw[:, slot, 0:n, :], ACT.Copy).then_inc(w_hi_ready, 1)

        def take(name, it, waits=()):
            b, v = scratch.task(name, it)
            act.wait_ge(full[b], v)
            for f, n in waits:
                act.wait_ge(flag(f), n)
            return b

        def func(out, in_, f, **kw):
            return act.activation(out, in_, f, **kw)

        def small(name, it, h, r):
            n = None if h is None else h + 1
            m = None if r is None else r + 1
            if name in ("ssq_q", "ssq_k", "ssq_a", "ssq_r"):
                b = take(name, it)
                count = DK if name in ("ssq_q", "ssq_k") else P
                if name == "ssq_k":
                    act.wait_ge(flag("zn_done"), h * 2 + 1)
                elif name == "ssq_r":
                    if h is not None:
                        act.wait_ge(flag("zn_done"), h * 2 + 2)
                elif name == "ssq_a":
                    if r is not None:
                        act.wait_ge(flag("mix_r_done"), m)
                elif name == "ssq_q":
                    if h is not None and not isinstance(h, int):
                        act.wait_ge(flag("mix_a_done"), h)
                ln = func(two(rr[:, :]), m_wide(b), ACT.Ln, scale=1.0 / count, bias=K("eps"))
                ln.then_inc(free[b], 1)
                act.wait_ge(free[b], scratch.task(name, it)[1])
                sig = {"ssq_q": "rr_q", "ssq_k": "rr_k", "ssq_a": "rr_a", "ssq_r": "rr_r"}[name]
                func(rr[:, :], rr[:, :], ACT.Exp, scale=-0.5).then_inc(flag(sig), 1)
            elif name in ("pages0", "pages1"):
                i = int(name[-1])
                b = take(name, it)
                func(kT[:, i * 4:(i + 1) * 4, 0:PAST], pages_view(b), ACT.Copy).then_inc(free[b], 1)
            elif name in ("k_nat", "v_nat"):
                dst, outs = (k_nat, ("k_prompt", "k_sample")) if name == "k_nat" else (v_nat, ("v_prompt", "v_sample"))
                b = take(name, it)
                if not isinstance(h, int):
                    act.wait_ge(flag(f"{name}_out"), h * 32)
                act.activation(dst[:, 0:4, :], M[b][:, 0, :].rearrange("p (j d) -> p j d", j=4), ACT.Copy)
                act.activation(dst[0:NS, 4, :], M[b][0:NS, 1, 0:P], ACT.Copy).then_inc(free[b], 1)
                act.wait_ge(free[b], scratch.task(name, it)[1])
                pr = o[outs[0]][0, 0].rearrange("g t h d -> t g h d")[:, :, bass.ds(h, 1), :].rearrange("t g h d -> t g (h d)")
                act.dma_start(pr, dst[:, 0:4, :]).then_inc(flag(f"{name}_out"), 16)
                sa = o[outs[1]][0, :, 0, bass.ds(h, 1), :].rearrange("b h d -> b (h d)")
                act.dma_start(sa, dst[0:NS, 4, :]).then_inc(flag(f"{name}_out"), 16)
            elif name.startswith("score"):
                i = int(name[-1])
                w = (i + 1) * P
                act.wait_ge(flag("neg_max_done"), h * 4 + (i + 1))
                for m_ in range(2):
                    e = func(score[:, m_, 0:w], score[:, m_, 0:w], ACT.Exp, scale=SCALE, bias=neg_max[:, m_:m_ + 1],
                             accum_out=row_sum[:, m_:m_ + 1])
                e.then_inc(flag("exp_done"), 1)
                act.wait_ge(flag("row_lam_done"), h * 4 + (i + 1))
                func(score[:, 1, 0:w], score[:, 1, 0:w], ACT.Copy, scale=row_lam[:, 0:1]).then_inc(flag("second_done"), 1)
            elif name == "s_score":
                b = take(name, it, [("s_max_done", n)])
                func(s_p[:, :], M[b][0:16, 0, 0:CP], ACT.Exp, scale=SCALE, bias=s_stat[:, 1:2],
                     accum_out=s_stat[:, 2:3]).then_inc(free[b], 1)
            elif name in ("w0", "w1", "w2", "w3"):
                i = int(name[-1])
                b = take(name, it)
                func(wT[:, i * (i + 1) // 2:(i + 1) * (i + 2) // 2, :], M[b][:, 0, 0:(i + 1) * P].rearrange("p (j q) -> p j q", j=i + 1), ACT.Copy).then_inc(free[b], 1)
            elif name == "s_out":
                b = take(name, it)
                func(s_o[:, :], M[b][0:NS, 0, 0:P], ACT.Copy).then_inc(free[b], 1)
            elif name == "s_turn":
                b = take(name, it)
                func(oT[:, SEQ:T], M[b][:, 0, 0:NS], ACT.Copy).then_inc(free[b], 1)
            elif name == "att_out":
                b = take(name, it)
                func(oT[:, 0:SEQ], M[b][:, 0, :], ACT.Copy).then_inc(free[b], 1)
                act.wait_ge(free[b], scratch.task(name, it)[1])
                sb_, sv = scratch.task("s_turn", it)
                act.wait_ge(free[sb_], sv)
                func(sq[:, :], oT[:, :], ACT.Square).then_inc(flag("sq_a"), 1)
            elif name == "i_nat":
                b = take(name, it)
                func(i_nat[:, 0:4, :], M[b][:, 0, :].rearrange("p (j d) -> p j d", j=4), ACT.Copy).then_inc(flag("i_nat_done"), 1)
                func(i_nat[0:NS, 4, :], M[b][0:NS, 1, 0:P], ACT.Copy)
                func(ks_nat[:, :], M[b][0:NS, 1, P:2 * P], ACT.Copy).then_inc(free[b], 1)
            elif name == "kh_nat":
                b = take(name, it)
                func(kh_nat[:, :, :], M[b][:, 0, :].rearrange("p (j d) -> p j d", j=4), ACT.Copy).then_inc(free[b], 1)
            elif name in ("rnn0", "rnn1", "rnn2", "rnn3"):
                j = int(name[-1])
                b = take(name, it)
                func(r_o[:, j * P:(j + 1) * P], M[b][:, 0, 0:P], ACT.Copy).then_inc(free[b], 1)
            elif name == "s_rnn":
                b = take(name, it)
                func(r_o[:, SEQ:T], M[b][:, 0, 0:NS], ACT.Copy).then_inc(free[b], 1)
                act.wait_ge(free[b], scratch.task(name, it)[1])
                b3, v3 = scratch.task("rnn3", it)
                act.wait_ge(free[b3], v3)
                act.wait_ge(flag("s_state_out"), r * 16 + 16)
                func(mix_r[:, :], r_o[:, :], ACT.Square).then_inc(flag("sq_r"), 1)

        def write_mix(name, h, tile, row):
            act.wait_ge(flag(f"{name}_done"), h + 1)
            act.dma_start(mix_d[bass.ds(row, 1), :, :].rearrange("k p t -> p (k t)"), tile[:, :]).then_inc(flag(f"{name}_out"), 16)

        def step(plan, it, h, r):
            for s in range(HALVES):
                if s % 2 == 0 and (h is not None or s == 0):
                    j = s // 2 + 1
                    split((HEADS if h is None else h) * HEAD_CHUNKS + j, (HEADS if h is None else h) * len(BLOCKS) + j // 2, j % 2)
                if r is not None and s == 0:
                    act.wait_ge(*evacuated("f", r))
                    func(r_k[:, :], z_f[:, :], ACT.Sigmoid, scale=-1.0)
                    func(z_f[:, :], z_f[:, :], ACT.Sigmoid).then_inc(flag("sig_f"), 1)
                    act.wait_ge(*evacuated("g", r))
                    func(r_g[:, :], z_g[:, :], ACT.Sigmoid).then_inc(flag("sig_g"), 1)
                    act.wait_ge(flag("f_done"), r + 1)
                    func(r_kh[:, :], z_f[:, 0:SEQ], ACT.Ln).then_inc(flag("log_f"), 1)
                if r is not None and s == 1:
                    act.wait_ge(flag("scan_done"), r + 1)
                    func(r_e[:, :], r_b[:, :], ACT.Exp).then_inc(flag("exp_b"), 1)
                    act.wait_ge(flag("b_left"), r + 1)
                    func(r_kd[:, :], r_b[:, :], ACT.Exp, scale=-1.0).then_inc(flag("exp_nb"), 1)
                    func(r_kh[:, :], r_kh[:, :], ACT.Exp).then_inc(flag("exp_left"), 1)
                if h is not None and s == 4:
                    act.wait_ge(*evacuated("q", h))
                    func(sq[:, :], z_q[:, :], ACT.Square).then_inc(flag("sq_q"), 1)
                if h is not None and s == 8:
                    act.wait_ge(*evacuated("k", h))
                    func(sq[:, :], z_k[:, :], ACT.Square).then_inc(flag("sq_k"), 1)
                for name in plan[s]:
                    small(name, it, h, r)
                if h is not None and s == 8:
                    act.wait_ge(flag("q_rot_done"), h + 1)
                    for m_ in range(2):
                        e = func(q_map[:, m_, :], q_rot[:, 0:SEQ], ACT.Copy, scale=K("maps")[:, m_:m_ + 1])
                    e.then_inc(flag("q_map_done"), 1)
                if r is not None and s == 13:
                    act.wait_ge(*read("upd3", it))
                    act.dma_start(o["rnn_prompt"][0, 0, bass.ds(r, 1), :, :].rearrange("h k v -> k (h v)"), state[:, 0, 0, :]).then_inc(flag("state_out"), 16)
                if r is not None and s == 17:
                    act.wait_ge(*read("s_upd", it))
                    act.dma_start(o["rnn_sample"][0, :, bass.ds(r, 1), :, :].rearrange("b h k v -> k (b h) v"), s_state[:, :, :]).then_inc(flag("s_state_out"), 16)
                if r is not None and s == 21:
                    write_mix("mix_r", r, mix_r, r + HEADS)
                if r is not None and s == 3 and h is not None:
                    write_mix("mix_a", r, mix_a, r)
            if h is None:
                write_mix("mix_a", r, mix_a, r)
            if r is not None:
                act.wait_ge(flag("mix_r_out"), r * 16 + 16)

        def operand(k, src, gain, base):
            func(act_hi[:, k, :], src, ACT.Copy, scale=gain).then_inc(flag("act_hi_ready"), 1)

        def squares(n, slot, src, x_ready=None):
            if not isinstance(n, int) or n >= 2:
                act.wait_ge(flag("sq_sum_done"), n - 1)
            func(sqx[:, slot, :], src, ACT.Square).then_inc(flag("squares"), 1)

        def norm(name):
            b = take(name, 0)
            func(two(R[:, :]), m_wide(b), ACT.Ln, scale=1.0 / D, bias=K("eps")).then_inc(free[b], 1)
            act.wait_ge(free[b], scratch.task(name, 0)[1])
            func(R[:, :], R[:, :], ACT.Exp, scale=-0.5).then_inc(flag("R_ready"), 1)

        def product_of(base, it, per, c0, n):
            for j in range(n):
                x = c0 + j + 2
                split(it * per + (base + x), it * (per // 2) + ((base + x) // 2), x % 2)

        def visit(what, arg):
            if what == "early":
                for t in range(4):
                    b = take(f"x{t}0", 0)
                    func(xT0[:, 0:8, t * P:(t + 1) * P], M[b][:, :, :].rearrange("p a (y c) -> p (a y) c", y=4), ACT.Copy).then_inc(free[b], 1)
                b = take("xs", 0)
                func(xT0[:, :, SEQ:T], M[b][:, 0, 0:KT * NS].rearrange("p (y c) -> p y c", y=KT), ACT.Copy).then_inc(free[b], 1)
                act.wait_ge(free[b], scratch.task("xs", 0)[1])
                act.wait_ge(*read("x31", 0))
                act.dma_start(xt_d.rearrange("k p t -> p k t"), xT0[:, :, :]).then_inc(flag("xT_written"), 16)
                act.wait_ge(*read("rows_a", 0))
                act.wait_ge(*read("rows_b", 0))
                split(0, 0, 0)
                for k in range(KT):
                    operand(k, xT0[:, k, :], vec(ROWS_A["norm_mix"] + k), 0)
                for k in range(KT):
                    squares(k, k % 2, xT0[:, k, :])
                b = take("ssx", 0)
                func(two(R[:, :]), m_wide(b), ACT.Ln, scale=1.0 / D, bias=K("eps")).then_inc(free[b], 1)
                act.wait_ge(free[b], scratch.task("ssx", 0)[1])
                func(R[:, :], R[:, :], ACT.Exp, scale=-0.5).then_inc(flag("R_ready"), 1)
                act.wait_ge(flag("tables_in"), 16)
                act.wait_ge(flag("setup_a"), 4)
                func(lams[:, 2:4], lams[:, 0:2], ACT.Exp).then_inc(flag("setup_e"), 1)
                func(lbt[:, 0:2, :], lbt[:, 0:2, :], ACT.Exp).then_inc(flag("setup_e"), 1)
            elif what == "heads":
                plan, h0, h1 = arg
                if h0 == 0:
                    step(plan, 0, 0, None)
                elif h1 == HEADS:
                    with act.Fori(h0, h1) as h:
                        step(plan, h - 1, h, h - 1)
                else:
                    step(plan, 0, None, HEADS - 1)
            elif what == "out":
                act.wait_ge(w_used, C_OUT)
                for k in range(KT):
                    act.wait_ge(flag(f"mix_in{k}"), 16)
                    func(act_hi[:, k, :], xT[:, k, :], ACT.Copy).then_inc(flag("act_hi_ready"), 1)

                def out_product(it, x, n, slot):
                    product_of(C_OUT, it, 4, 2 * x, 2)
                    act.wait_ge(g_free[x], it + (g_out[x] + 1))
                    squares(n + KT, slot, column(xT, n))
                out_product(0, 0, 0, 0)
                b = take("p_turn", 0)
                func(pT[:, :, 0:SEQ], M[b][:, :, :], ACT.Copy).then_inc(free[b], 1)
                b = take("ps_turn", 0)
                func(pT[:, :, SEQ:T], M[b][:, 0, 0:2 * NS].rearrange("p (a c) -> p a c", a=2), ACT.Copy).then_inc(free[b], 1)
                for nm in ("p_turn", "ps_turn"):
                    b, v = scratch.task(nm, 0)
                    act.wait_ge(free[b], v)
                func(pT_hi[:, :, :], pT[:, :, :], ACT.Copy).then_inc(flag("pT_hi_done"), 1)
                out_product(0, 1, 1, 1)
                with act.Fori(1, KT // 2) as it:
                    for x in range(2):
                        out_product(it, x, it * 2 + x, x)
                for k in range(KT):
                    act.wait_ge(w_used, C_FFN)
                    if k >= KT - 2:
                        act.wait_ge(g_free[k % 2], g_ffn[k % 2])
                    operand(k, xT[:, k, :], vec(ROWS_A["norm_ffn"] + k), 0)
                norm("ss_out")
            elif what == "ffn":
                with act.Fori(0, GROUPS) as g:
                    def ff_block(f, first):
                        n = g * GF + f
                        cb, c2 = C_FFN, C_FFN // 2

                        def two_chunks(x):
                            for j in (2 * x + 2, 2 * x + 3):
                                split(g * GROUP_CHUNKS + f * 4 + (cb + j), g * (GROUP_CHUNKS // 2) + f * 2 + (c2 + j // 2), j % 2)
                        two_chunks(0)
                        if first:
                            b = take("c_old", g)
                            func(conv_old[:, :, :, :].rearrange("p f b w -> p (f b w)"), M[b][:, 0, 0:GF * 16], ACT.Copy).then_inc(free[b], 1)
                        act.wait_ge(flag("ffc_done"), n + 1)
                        func(ffs[:, :], ffc[:, :], ACT.Silu).then_inc(flag("silu_done"), 1)
                        two_chunks(1)
                        act.wait_ge(flag("ffu_done"), n + 1)
                        func(column(u_hi, f), ffu[:, :], ACT.Copy).then_inc(flag("u_hi_done"), 1)
                        b = take("c_new", n)
                        act.wait_ge(flag("conv_out"), g * 32 + 16)
                        func(conv_new[:, bass.ds(f * P, P)], M[b][0:10, 0, 0:P], ACT.Copy).then_inc(free[b], 1)

                    ff_block(0, True)
                    with act.Fori(1, GF) as f:
                        ff_block(f, False)
                    act.wait_ge(free[1], scratch.task("c_new", g * GF)[1] + (GF - 1))
                    cols = bass.ds(g * (GF * P), GF * P)
                    act.dma_start(o["conv_prompt"][0, 0, :, cols], conv_new[0:2, :]).then_inc(flag("conv_out"), 16)
                    act.dma_start(o["conv_sample"][0, :, 1, cols], conv_new[2:10, :]).then_inc(flag("conv_out"), 16)
                    with act.Fori(0, KT // 2) as m:
                        for x in range(2):
                            for j in (2 * x + 2, 2 * x + 3):
                                split(g * GROUP_CHUNKS + m * 4 + (C_FFN + FF_CHUNKS + j), g * (GROUP_CHUNKS // 2) + m * 2 + ((C_FFN + FF_CHUNKS) // 2 + j // 2), j % 2)
                            act.wait_ge(g_free[x], g * g_per_group + m + (g_ffn[x] + GF + 1))
                            squares(g * KT + m * 2 + (2 * KT + x), x, column(xT, m * 2 + x))
            elif what == "mid":
                for k in range(KT):
                    act.wait_ge(w_used, C_PLE)
                    if k >= KT - 2:
                        act.wait_ge(g_free[k % 2], g_ple[k % 2])
                    operand(k, xT[:, k, :], vec(ROWS_A["norm_ple"] + k), 0)
                norm("ss_ffn")
            elif what == "ple":
                def sp_(m, j):
                    c2 = (0, 0, 2, 1, 3, 3)[j % 6] + 4 * (j // 6)
                    split(m * 6 + (C_PLE + j), m * 4 + (C_PLE // 2 + c2), j % 2, GATE_TILES)

                def y_out(x, m):
                    n = m * 2 + x
                    b = take(f"y{x}", m)
                    if not isinstance(m, int) or m > 0:
                        act.wait_ge(flag(f"y_out{x}"), m * 32)
                    func(y_nat[:, x, 0:4, :], M[b][:, 0, :].rearrange("p (j d) -> p j d", j=4), ACT.Copy)
                    func(y_nat[0:NS, x, 4, :], M[b][0:NS, 1, 0:P], ACT.Copy).then_inc(free[b], 1)
                    act.wait_ge(free[b], scratch.task(f"y{x}", m)[1])
                    cols = bass.ds(n * P, P)
                    act.dma_start(o["y_prompt"][0].rearrange("(j p) d -> p j d", p=P)[:, :, cols], y_nat[:, x, 0:4, :]).then_inc(flag(f"y_out{x}"), 16)
                    act.dma_start(o["y_sample"][:, 0, cols], y_nat[0:NS, x, 4, :]).then_inc(flag(f"y_out{x}"), 16)

                def ple(m, x, before, last=False):
                    sp_(m, 3 * x + 2)
                    if before is not None:
                        y_out(*before)
                    if not last:
                        sp_(m, 3 * x + 3)
                        sp_(m, 3 * x + 4)
                    act.wait_ge(g_free[x], m + (g_ple[x] + 1))
                    func(gate[:, :], gate[:, :], ACT.Sigmoid).then_inc(flag("gate_done"), 1)

                ple(0, 0, None)
                ple(0, 1, (0, 0))
                with act.Fori(1, KT // 2 - 1) as m:
                    ple(m, 0, (1, m - 1))
                    ple(m, 1, (0, m))
                m = KT // 2 - 1
                ple(m, 0, (1, m - 1))
                ple(m, 1, (0, m), last=True)
                y_out(1, m)

        phases(visit)

    @block.vector
    def _(dve):
        def low(c, slot, n=KC):
            dve.wait_ge(w_hi_ready, c + 1)
            dve.tensor_tensor(flat(w_lo[:, slot, 0:n, :]), flat(w_raw[:, slot, 0:n, :]), flat(w_hi[:, slot, 0:n, :]).bitcast(F32),
                              ALU.subtract).then_inc(w_lo_ready, 1)

        def take(name, it, waits=()):
            b, v = scratch.task(name, it)
            dve.wait_ge(full[b], v)
            for f, n in waits:
                dve.wait_ge(flag(f), n)
            return b

        def evacuate(name, h, z):
            blk = BLOCKS.index(name)
            dve.wait_ge(w_used, h * HEAD_CHUNKS + 2 * blk + 2)
            dve.tensor_tensor(two(z[:, :]), G[blk % 2][:, :, 0:TH], two(R[:, :]), ALU.mult).then_inc(g_free[blk % 2], 1)

        def small(name, it, h, r):
            n = None if h is None else h + 1
            m = None if r is None else r + 1
            if name in ("ssq_q", "ssq_k"):
                z, gain, i = (z_q, ROWS_A["q"], 1) if name == "ssq_q" else (z_k, ROWS_A["k"], 2)
                dve.wait_ge(flag("rr_q" if i == 1 else "rr_k"), n)
                dve.scalar_tensor_tensor(zn[:, :], z[:, :], vec(gain), rr[:, :], ALU.mult, ALU.mult).then_inc(flag("zn_done"), 1)
                dve.wait_ge(flag("zn_done"), h * 2 + i)
                dve.tensor_tensor(z[:, :], zn[:, :], K("cos"), ALU.mult).then_inc(flag("cos_done"), 1)
            elif name in ("rot_q", "rot_k"):
                z, dst, i, sig = (z_q, q_rot, 1, "q_rot_done") if name == "rot_q" else (z_k, k_rot, 2, "k_rot_done")
                b = take(name, it)
                dve.tensor_tensor(two(rot[:, :]), m_wide(b), two(K("sin")), ALU.mult).then_inc(free[b], 1)
                dve.wait_ge(free[b], scratch.task(name, it)[1])
                dve.wait_ge(flag("cos_done"), h * 2 + i)
                dve.tensor_tensor(dst[:, :], z[:, :], rot[:, :], ALU.add).then_inc(flag(sig), 1)
                dve.wait_ge(flag(sig), n)
                if name == "rot_q":
                    dve.tensor_tensor(q_pad[:, :, :], q_rot[:, SEQ:T].unsqueeze(2).broadcast_to([P, NS, 16]),
                                      K("pad_q").rearrange("p (b c) -> p b c", b=NS), ALU.mult).then_inc(flag("q_pad_done"), 1)
                else:
                    dve.tensor_copy(kT[:, :, PAST:PAST + 1].rearrange("p b o -> p (b o)"), k_rot[:, SEQ:T]).then_inc(flag("kT_new_done"), 1)
            elif name == "v_nat":
                dve.wait_ge(*evacuated("v", h))
                dve.tensor_copy(v_two[:, :].rearrange("p (b w) -> p b w", w=2),
                                z_v[:, SEQ:T].unsqueeze(2).broadcast_to([P, NS, 2])).then_inc(flag("v_two_done"), 1)
            elif name.startswith("score"):
                i = int(name[-1])
                w = (i + 1) * P
                c = h * 4 + (i + 1)
                b = take(name, it)
                if i > 0 or not isinstance(h, int):
                    dve.wait_ge(flag("wgt_done"), c - 1)
                dve.memset(neg_max[:, :], 0.0)
                for m_ in range(2):
                    t = dve.tensor_tensor_reduce(score[:, m_, 0:w], M[b][:, m_, 0:w], K("causal")[:, SEQ - w:SEQ], 1.0, -3e38,
                                                 ALU.add, ALU.max, row_max[:, m_:m_ + 1])
                t.then_inc(free[b], 1)
                dve.wait_ge(free[b], scratch.task(name, it)[1])
                dve.tensor_scalar(neg_max[:, :], row_max[:, :], -SCALE, None, ALU.mult).then_inc(flag("neg_max_done"), 1)
                dve.wait_ge(flag("exp_done"), c)
                dve.reciprocal(row_inv[:, :], row_sum[:, :]).then_inc(flag("row_inv_done"), 1)
                dve.wait_ge(flag("row_inv_done"), c)
                dve.tensor_tensor(row_lam[:, :], row_inv[:, 1:2], lam[:, :], ALU.mult).then_inc(flag("row_lam_done"), 1)
                dve.wait_ge(flag("second_done"), c)
                if i > 0:
                    b2, v2 = scratch.task(f"w{i - 1}", it)
                    dve.wait_ge(full[b2], v2)
                dve.scalar_tensor_tensor(wgt[:, 0:w], score[:, 0, 0:w], row_inv[:, 0:1], score[:, 1, 0:w],
                                         ALU.mult, ALU.subtract).then_inc(flag("wgt_done"), 1)
            elif name == "s_score":
                b = take(name, it)
                dve.tensor_reduce(s_stat[:, 0:1], M[b][0:16, 0, 0:CP], AX.X, ALU.max).then_inc(flag("s_raw_max"), 1)
                dve.wait_ge(flag("s_raw_max"), n)
                dve.tensor_scalar(s_stat[:, 1:2], s_stat[:, 0:1], -SCALE, None, ALU.mult).then_inc(flag("s_max_done"), 1)
                dve.wait_ge(*read(name, it))
                dve.reciprocal(s_stat[:, 3:4], s_stat[:, 2:3]).then_inc(flag("s_inv"), 1)
                dve.wait_ge(flag("s_inv"), n)
                dve.tensor_tensor(s_stat[:, 4:5], s_stat[:, 3:4], coef[:, :], ALU.mult).then_inc(flag("s_coef"), 1)
                dve.wait_ge(flag("s_coef"), n)
                dve.tensor_scalar(s_p[:, :], s_p[:, :], s_stat[:, 4:5], None, ALU.mult).then_inc(flag("s_p_done"), 1)
                dve.wait_ge(flag("s_p_done"), n)
                dve.tensor_scalar(new_w[0:16, :], K("pairs")[0:16, :], s_p[:, PAST:PAST + 1], None, ALU.mult).then_inc(flag("new_w_done"), 1)
            elif name == "s_prob":
                b = take(name, it)
                dve.tensor_reduce(w_sum[:, :], M[b][:, 0, 0:32].rearrange("p (x w) -> p x w", w=2), AX.X, ALU.add).then_inc(flag("w_sum_done"), 1)
                dve.tensor_copy(new_v[0:16, :], M[b][0:16, 1, 0:P]).then_inc(free[b], 1)
                dve.wait_ge(flag("w_sum_done"), n)
                wp = w_pad[:, :, :].rearrange("p (b g) c -> p b g c", g=2)
                for g in range(2):
                    t = dve.tensor_tensor(wp[:, :, g, :], w_sum[:, g * NS:(g + 1) * NS].unsqueeze(2).broadcast_to([P, NS, NS]),
                                          K("delta8").rearrange("p (b c) -> p b c", b=NS), ALU.mult)
                t.then_inc(flag("w_pad_done"), 1)
            elif name == "ssq_a":
                dve.wait_ge(flag("rr_a"), n)
                if not isinstance(h, int):
                    dve.wait_ge(flag("mix_a_out"), h * 16)
                dve.scalar_tensor_tensor(mix_a[:, :], oT[:, :], gain_a[:, 0:1], rr[:, :], ALU.mult, ALU.mult).then_inc(flag("mix_a_done"), 1)
            elif name == "intra":
                b = take(name, it)
                dve.tensor_tensor(intra[:, :, :], M[b][:, 0, :].rearrange("p (j t) -> p j t", j=4),
                                  K("chunk_pairs").unsqueeze(1).broadcast_to([P, 4, P]), ALU.mult).then_inc(free[b], 1)
            elif name.startswith("upd"):
                j = int(name[-1])
                b = take(name, it)
                for c in range(CPB):
                    x = j * CPB + c
                    u = M[b][:, c // 4, (c % 4) * P:(c % 4 + 1) * P]
                    dst = state[:, j % 2, c + 1, :] if c < CPB - 1 else state[:, (j + 1) % 2, 0, :]
                    if c == CPB - 1 and j > 0:
                        b2, v2 = scratch.task(f"rnn{j - 1}", it)
                        dve.wait_ge(full[b2], v2)
                    if x == 0:
                        t = dve.tensor_copy(dst, u)
                    else:
                        if c == 0:
                            dve.wait_ge(*read(f"upd{j - 1}", it))
                        else:
                            dve.wait_ge(flag("state_done"), r * 28 + (j * 7 + c))
                        t = dve.scalar_tensor_tensor(dst, state[:, j % 2, c, :], r_e[:, x * CHUNK + CHUNK - 1:x * CHUNK + CHUNK], u, ALU.mult, ALU.add)
                    if c < CPB - 1:
                        t.then_inc(flag("state_done"), 1)
                    else:
                        t.then_inc(free[b], 1)
                if j == 3:
                    dve.wait_ge(*read("i_nat", it))
                    dve.tensor_tensor(s_iexp[:, :, :], i_nat[0:NS, 4:5, :].broadcast_to([NS, NS, P]),
                                      K("delta_p")[0:NS, :].unsqueeze(2).broadcast_to([NS, NS, P]), ALU.mult).then_inc(flag("s_iexp_done"), 1)
            elif name == "s_upd":
                b = take(name, it, [("f_s_done", m), ("s_state_in", r * 16 + 16)])
                for y in range(NS):
                    t = dve.scalar_tensor_tensor(s_state[:, y, :], s_state[:, y, :], f_s[:, y:y + 1],
                                                 M[b][:, y // 4, (y % 4) * P:(y % 4 + 1) * P], ALU.mult, ALU.add)
                t.then_inc(free[b], 1)
            elif name == "ssq_r":
                dve.wait_ge(flag("rr_r"), m)
                dve.scalar_tensor_tensor(r_o[:, :], r_o[:, :], vec(ROWS_A["rnn"]), rr[:, :], ALU.mult, ALU.mult).then_inc(flag("r_normed"), 1)
                dve.wait_ge(flag("r_normed"), m)
                dve.wait_ge(flag("r_gate"), m)
                dve.tensor_tensor(mix_r[:, :], r_o[:, :], z_g[:, :], ALU.mult).then_inc(flag("mix_r_done"), 1)

        def step(plan, it, h, r):
            for s in range(HALVES):
                if h is not None and s % 4 == 0 and s > 0:
                    name = BLOCKS[s // 4 - 1]
                    evacuate(name, h, {"q": z_q, "k": z_k, "v": z_v, "f": z_f, "i": z_i, "r": z_r}[name])
                if r is not None and s == 0:
                    evacuate("g", r, z_g)
                if s % 2 == 0 and (h is not None or s == 0):
                    j = s // 2 + 1
                    low((HEADS if h is None else h) * HEAD_CHUNKS + j, j % 2)
                if r is not None and s == 0:
                    dve.wait_ge(flag("sig_f"), r + 1)
                    dve.tensor_scalar(z_f[:, :], z_f[:, :], oml[:, bass.ds(r, 1)], lb[:, bass.ds(r, 1)], ALU.mult, ALU.add).then_inc(flag("f_done"), 1)
                    dve.wait_ge(flag("f_done"), r + 1)
                    dve.tensor_copy(f_s[:, :], z_f[:, SEQ:T]).then_inc(flag("f_s_done"), 1)
                    dve.tensor_scalar(r_k[:, :], r_k[:, :], oml[:, bass.ds(r, 1)], None, ALU.mult).then_inc(flag("r_k_done"), 1)
                    dve.wait_ge(flag("sig_g"), r + 1)
                    dve.tensor_tensor(z_g[:, :], z_g[:, :], r_g[:, :], ALU.mult).then_inc(flag("r_gate"), 1)
                    dve.wait_ge(flag("log_f"), r + 1)
                    dve.tensor_tensor_scan(r_b[:, :], K("restart"), r_kh[:, :], 0.0, ALU.mult, ALU.add).then_inc(flag("scan_done"), 1)
                    dve.wait_ge(flag("scan_done"), r + 1)
                    rb = r_b[:, :].rearrange("p (c t) -> p c t", t=CHUNK)
                    dve.tensor_tensor(r_kh[:, :].rearrange("p (c t) -> p c t", t=CHUNK),
                                      rb[:, :, CHUNK - 1:CHUNK].broadcast_to([P, NCH, CHUNK]), rb, ALU.subtract).then_inc(flag("b_left"), 1)
                for name in plan[s]:
                    small(name, it, h, r)
            if r is not None:
                dve.wait_ge(flag("state_out"), r * 16 + 16)
                dve.wait_ge(flag("mix_r_out"), r * 16 + 16)

        def operand(k, src, gain, n):
            dve.wait_ge(flag("act_hi_ready"), n)
            dve.scalar_tensor_tensor(act_lo[:, k, :], src, gain, act_hi[:, k, :].bitcast(F32), ALU.mult, ALU.subtract).then_inc(flag("act_lo_ready"), 1)

        def add_squares(n, slot):
            dve.wait_ge(flag("squares"), n + 1)
            if not isinstance(n, int) or n > 0:
                dve.wait_ge(flag("sq_sum_done"), n)
            dve.tensor_tensor(sq_sum[:, :], sq_sum[:, :], sqx[:, slot, :], ALU.add).then_inc(flag("sq_sum_done"), 1)

        def zero_sum(n):
            dve.memset(sq_sum[:, :], 0.0).then_inc(flag("sum_zeroed"), 1)
            dve.wait_ge(flag("sum_zeroed"), n)

        def pad(it):
            if scratch.padded:
                b = take("pad", it)
                dve.tensor_copy(pad_out[:, :], M[b][0:32, 0, 0:1]).then_inc(free[b], 1)

        def visit(what, arg):
            if what == "early":
                for t in range(4):
                    b = take(f"x{t}1", 0)
                    dve.tensor_copy(xT0[:, 8:16, t * P:(t + 1) * P], M[b][:, :, :].rearrange("p a (y c) -> p (a y) c", y=4)).then_inc(free[b], 1)
                b = take("rows_a", 0)
                dve.tensor_copy(vecs[:, 0:NROWS_A], M[b][:, 0, 0:NROWS_A]).then_inc(free[b], 1)
                b = take("rows_b", 0)
                dve.tensor_copy(vecs[:, NROWS_A:NCOLS], M[b][:, 0, 0:4 * FB]).then_inc(free[b], 1)
                dve.wait_ge(*read("rows_a", 0))
                dve.wait_ge(*read("rows_b", 0))
                low(0, 0)
                for k in range(KT):
                    operand(k, xT0[:, k, :], vec(ROWS_A["norm_mix"] + k), k + 1)
                zero_sum(1)
                for k in range(KT):
                    add_squares(k, k % 2)
                dve.wait_ge(flag("xT_written"), 16)
                dve.wait_ge(flag("tables_in"), 16)
                dve.wait_ge(flag("lam_in"), 64)
                for i in range(2):
                    dve.tensor_tensor_reduce(lamv[:, 2 * i, :], lamv[:, 2 * i, :], lamv[:, 2 * i + 1, :], 1.0, 0.0,
                                             ALU.mult, ALU.add, lams[:, i:i + 1]).then_inc(flag("setup_a"), 1)
                rows = [vec(ROWS_A[x], HEADS) for x in ("lb0", "lb1")]
                dve.tensor_tensor(lbt[:, 2, :], rows[0], rows[1], ALU.max).then_inc(flag("lb_max"), 1)
                dve.wait_ge(flag("lb_max"), 1)
                for i in range(2):
                    dve.tensor_tensor(lbt[:, i, :], rows[i], lbt[:, 2, :], ALU.subtract).then_inc(flag("setup_a"), 1)
                dve.wait_ge(flag("setup_e"), 2)
                dve.tensor_tensor(lam[:, :], lams[:, 2:3], lams[:, 3:4], ALU.subtract).then_inc(flag("setup_d"), 1)
                dve.wait_ge(flag("setup_d"), 1)
                dve.tensor_scalar(lam[:, :], lam[:, :], LAM_INIT, None, ALU.add).then_inc(flag("setup_d"), 1)
                dve.wait_ge(flag("setup_d"), 2)
                dve.scalar_tensor_tensor(coef[:, :], K("coef")[0:16, 1:2], lam[0:16, 0:1], K("coef")[0:16, 0:1], ALU.mult, ALU.add).then_inc(flag("setup_d"), 1)
                dve.tensor_tensor(lbt[:, 2, :], lbt[:, 0, :], lbt[:, 1, :], ALU.add).then_inc(flag("setup_d"), 1)
                dve.wait_ge(flag("setup_d"), 4)
                dve.reciprocal(lbt[:, 1, :], lbt[:, 2, :]).then_inc(flag("setup_d"), 1)
                dve.wait_ge(flag("setup_d"), 5)
                dve.tensor_tensor(lb[:, :], lbt[:, 0, :], lbt[:, 1, :], ALU.mult).then_inc(flag("setup_d"), 1)
                dve.wait_ge(flag("setup_d"), 6)
                dve.tensor_scalar(oml[:, :], lb[:, :], -1.0, 1.0, ALU.mult, ALU.add).then_inc(flag("setup_d"), 1)
                dve.tensor_scalar(gain_a[:, :], vec(ROWS_A["att"]), 1.0 - LAM_INIT, None, ALU.mult).then_inc(flag("setup_d"), 1)
                dve.wait_ge(flag("setup_d"), 8)
                dve.wait_ge(flag("R_ready"), 1)
                dve.wait_ge(flag("zeros_set"), 2)
            elif what == "heads":
                plan, h0, h1 = arg
                if h0 == 0:
                    step(plan, 0, 0, None)
                elif h1 == HEADS:
                    with dve.Fori(h0, h1) as h:
                        step(plan, h - 1, h, h - 1)
                else:
                    step(plan, 0, None, HEADS - 1)
            elif what == "out":
                for k in range(KT):
                    dve.wait_ge(flag("act_hi_ready"), KT + k + 1)
                    dve.tensor_tensor(act_lo[:, k, :], xT[:, k, :], act_hi[:, k, :].bitcast(F32), ALU.subtract).then_inc(flag("act_lo_ready"), 1)
                zero_sum(2)

                def out_product(it, x, n):
                    low(it * 4 + (C_OUT + 2 * x + 2), 0)
                    dve.wait_ge(w_used, it * 4 + (C_OUT + 2 * x + 2))
                    dve.tensor_tensor(two(column(xT, n)), G[x][:, :, 0:TH], two(column(xT, n)), ALU.add).then_inc(g_free[x], 1)
                    low(it * 4 + (C_OUT + 2 * x + 3), 1)
                    add_squares(n + KT, x)
                dve.wait_ge(flag("x_back"), KT * 16)
                out_product(0, 0, 0)
                dve.wait_ge(flag("pT_hi_done"), 1)
                dve.tensor_tensor(pT_lo[:, :, :], pT[:, :, :], pT_hi[:, :, :].bitcast(F32), ALU.subtract).then_inc(flag("pT_lo_done"), 1)
                out_product(0, 1, 1)
                with dve.Fori(1, KT // 2) as it:
                    for x in range(2):
                        out_product(it, x, it * 2 + x)
                pad(0)
                for k in range(KT):
                    operand(k, xT[:, k, :], vec(ROWS_A["norm_ffn"] + k), 2 * KT + k + 1)
                dve.wait_ge(flag("R_ready"), 2)
            elif what == "ffn":
                dve.memset(ffg[:, 0:2], 0.0).then_inc(flag("conv_zero"), 1)
                dve.wait_ge(flag("conv_zero"), 1)
                with dve.Fori(0, GROUPS) as g:
                    with dve.Fori(0, GF) as f:
                        n = g * GF + f
                        c0 = g * GROUP_CHUNKS + f * 4

                        def w(i):
                            return vecs[:, bass.ds(n + COL_CW[i], 1)]

                        def linked(ins, v):
                            ins.then_inc(flag("ff_step"), 1)
                            dve.wait_ge(flag("ff_step"), n * FF_STEPS + v)
                        low(c0 + (C_FFN + 2), 0)
                        dve.wait_ge(w_used, c0 + (C_FFN + 2))
                        b, v = scratch.task("c_new", n)
                        dve.wait_ge(full[b], v - 1)
                        dve.tensor_tensor(two(ffg[:, 2:T + 2]), G[0][:, :, 0:TH], two(R[:, :]), ALU.mult).then_inc(g_free[0], 1)
                        low(c0 + (C_FFN + 3), 1)
                        dve.wait_ge(g_free[0], g * g_per_group + f + (g_ffn[0] + 1))
                        linked(dve.tensor_scalar(ffc[:, :], ffg[:, 2:T + 2], w(2), w(3), ALU.mult, ALU.add), 1)
                        linked(dve.scalar_tensor_tensor(ffc[:, 0:SEQ], ffg[:, 1:SEQ + 1], w(1), ffc[:, 0:SEQ], ALU.mult, ALU.add), 2)
                        linked(dve.scalar_tensor_tensor(ffc[:, 0:SEQ], ffg[:, 0:SEQ], w(0), ffc[:, 0:SEQ], ALU.mult, ALU.add), 3)
                        cb, cv = scratch.task("c_old", g)
                        dve.wait_ge(free[cb], cv)
                        old = conv_old[:, bass.ds(f, 1), :, :].rearrange("p f b w -> p (f b) w")
                        past = [old[:, :, i:i + 1].rearrange("p b o -> p (b o)") for i in range(2)]
                        linked(dve.scalar_tensor_tensor(ffc[:, SEQ:T], past[1], w(1), ffc[:, SEQ:T], ALU.mult, ALU.add), 4)
                        dve.scalar_tensor_tensor(ffc[:, SEQ:T], past[0], w(0), ffc[:, SEQ:T], ALU.mult, ALU.add).then_inc(flag("ffc_done"), 1)
                        low(c0 + (C_FFN + 4), 0)
                        dve.wait_ge(w_used, c0 + (C_FFN + 4))
                        dve.tensor_tensor(two(ffu[:, :]), G[1][:, :, 0:TH], two(R[:, :]), ALU.mult).then_inc(g_free[1], 1)
                        low(c0 + (C_FFN + 5), 1)
                        dve.wait_ge(g_free[1], g * g_per_group + f + (g_ffn[1] + 1))
                        dve.wait_ge(flag("silu_done"), n + 1)
                        dve.tensor_tensor(ffu[:, :], ffu[:, :], ffs[:, :], ALU.mult).then_inc(flag("ffu_done"), 1)
                        dve.wait_ge(flag("u_hi_done"), n + 1)
                        dve.tensor_tensor(column(u_lo, f), ffu[:, :], column(u_hi, f).bitcast(F32), ALU.subtract).then_inc(flag("u_done"), 1)
                    dve.memset(sq_sum[:, :], 0.0).then_inc(flag("sum_zeroed"), 1)
                    with dve.Fori(0, KT // 2) as m:
                        for x in range(2):
                            c0 = g * GROUP_CHUNKS + m * 4
                            low(c0 + (C_FFN + FF_CHUNKS + 2 * x + 2), 0)
                            dve.wait_ge(w_used, c0 + (C_FFN + FF_CHUNKS + 2 * x + 2))
                            col = column(xT, m * 2 + x)
                            dve.tensor_tensor(two(col), G[x][:, :, 0:TH], two(col), ALU.add).then_inc(g_free[x], 1)
                            low(c0 + (C_FFN + FF_CHUNKS + 2 * x + 3), 1)
                            dve.wait_ge(flag("sum_zeroed"), g + 3)
                            add_squares(g * KT + m * 2 + (2 * KT + x), x)
            elif what == "mid":
                pad(0)
                for k in range(KT):
                    operand(k, xT[:, k, :], vec(ROWS_A["norm_ple"] + k), 3 * KT + k + 1)
                dve.wait_ge(flag("R_ready"), 3)
            elif what == "ple":
                def ple(m, x, last=False):
                    n = m * 2 + x
                    c = C_PLE + 3 * x
                    low(m * 6 + (c + 2), x % 2, GATE_TILES)
                    if not last:
                        low(m * 6 + (c + 3), (x + 1) % 2, GATE_TILES)
                    dve.wait_ge(w_used, m * 6 + (c + 3))
                    dve.tensor_tensor(two(gate[:, :]), G[x][:, :, 0:TH], two(R[:, :]), ALU.mult).then_inc(g_free[x], 1)
                    if not last:
                        low(m * 6 + (c + 4), x % 2, GATE_TILES)
                    b = take(f"pp{x}", m)
                    dve.wait_ge(flag("gate_done"), n + 1)
                    dve.tensor_tensor(two(gate[:, :]), m_wide(b), two(gate[:, :]), ALU.mult).then_inc(free[b], 1)
                    dve.wait_ge(free[b], scratch.task(f"pp{x}", m)[1])
                    if not isinstance(m, int) or m > 0:
                        b, v = scratch.task(f"y{x}", m)
                        dve.wait_ge(full[b], v - 2)
                    dve.tensor_tensor(y_t[:, x, :], column(xT, n), gate[:, :], ALU.add).then_inc(flag("y_done"), 1)

                ple(0, 0)
                ple(0, 1)
                with dve.Fori(1, KT // 2 - 1) as m:
                    for x in range(2):
                        ple(m, x)
                ple(KT // 2 - 1, 0)
                ple(KT // 2 - 1, 1, last=True)

        phases(visit)

    @block.gpsimd
    def _(pool):
        def step(plan, it, h, r):
            if r is None:
                return
            pool.wait_ge(flag("exp_nb"), r + 1)
            pool.wait_ge(flag("r_k_done"), r + 1)
            nc.gpsimd.tensor_tensor(r_kd[:, :], r_k[:, 0:SEQ], r_kd[:, :], ALU.mult).then_inc(flag("r_kd_done"), 1)
            nc.gpsimd.tensor_tensor(r_qd, z_r[:, 0:SEQ], r_e[:, :], ALU.mult).then_inc(flag("r_qd_done"), 1)
            pool.wait_ge(flag("exp_left"), r + 1)
            nc.gpsimd.tensor_tensor(r_kh[:, :], r_k[:, 0:SEQ], r_kh[:, :], ALU.mult).then_inc(flag("r_kh_done"), 1)
            pool.wait_ge(flag("i_nat_done"), r + 1)
            for j in range(4):
                if j > 0:
                    b, v = scratch.task(f"upd{j - 1}", it)
                    pool.wait_ge(full[b], v)
                nc.gpsimd.tensor_tensor(v_chunks[:, :, :], i_nat[:, j:j + 1, :].broadcast_to([P, CPB, P]),
                                        K("chunk_of").unsqueeze(2).broadcast_to([P, CPB, P]), ALU.mult).then_inc(flag("v_chunks_done"), 1)

        def visit(what, arg):
            if what == "early":
                pool.wait_ge(flag("xT_written"), 16)
                pool.wait_ge(flag("act_lo_ready"), KT)
                pool.wait_ge(flag("sq_sum_done"), KT)
                pool.wait_ge(flag("tables_in"), 16)
                nc.gpsimd.memset(new_w[:, :], 0.0).then_inc(flag("zeros_set"), 1)
                nc.gpsimd.memset(new_v[:, :], 0.0).then_inc(flag("zeros_set"), 1)
            elif what == "heads":
                plan, h0, h1 = arg
                if h0 == 0:
                    return
                if h1 == HEADS:
                    with pool.Fori(h0, h1) as h:
                        step(plan, h - 1, h, h - 1)
                else:
                    step(plan, 0, None, HEADS - 1)

        phases(visit)

    ctx.close()


_INS = ["x_prompt", "x_sample", "p_prompt", "p_sample", "cache_k", "cache_v", "state_rnn", "state_ffn_conv", "page_table",
        "norm_mix", "w_in", "q_norm", "k_norm", "lam_q1", "lam_k1", "lam_q2", "lam_k2", "att_out_norm", "rnn_out_norm",
        "lower_bounds", "w_out", "norm_ffn", "w_gate", "w_up", "conv_w", "conv_b", "w_down", "norm_ple", "w_ple_gate",
        "w_ple_proj"]
_OUTS = {
    "y_prompt": (1, SEQ, D),
    "y_sample": (NS, 1, D),
    "k_prompt": (1, 1, SEQ // PAGE, PAGE, HEADS, P),
    "v_prompt": (1, 1, SEQ // PAGE, PAGE, HEADS, P),
    "rnn_prompt": (1, 1, HEADS, P, P),
    "conv_prompt": (1, 1, 2, D_FF),
    "k_sample": (1, NS, 1, HEADS, P),
    "v_sample": (1, NS, 1, HEADS, P),
    "rnn_sample": (1, NS, HEADS, P, P),
    "conv_sample": (1, NS, 2, D_FF),
}


def kernel(**inputs):
    import concourse.bacc as bacc
    from concourse.bass_utils import run_bass_kernel_spmd as run

    nc = bacc.Bacc("TRN2", target_bir_lowering=False, num_devices=1)
    arrays, a, o = {}, {}, {}
    for name in _INS + ["consts"]:
        x = constants() if name == "consts" else np.ascontiguousarray(inputs[name])
        arrays[f"in_{name}"] = x
        a[name] = nc.dram_tensor(f"in_{name}", x.shape, mybir.dt.from_np(x.dtype), kind="ExternalInput").ap()
    for name, shape in _OUTS.items():
        o[name] = nc.dram_tensor(f"out_{name}", shape, F32, kind="ExternalOutput").ap()
    program(nc, a, o)
    r = run(nc, [arrays], core_ids=[0])
    return tuple(r.results[0][f"out_{name}"] for name in _OUTS)
```

```python
from contextlib import ExitStack

import numpy as np

import concourse.bass as bass
from concourse import mybir

F32 = mybir.dt.float32
F32R = mybir.dt.float32r
I32 = mybir.dt.int32
ALU = mybir.AluOpType
ACT = mybir.ActivationFunctionType
AX = mybir.AxisListType

P = 128
D = 2048
SEQ = 512
NS = 8
T = SEQ + NS
TH = T // 2
KT = D // P
HEADS = 8
DK = 64
PAGE = 128
PAGES = 2
NPG = NS * PAGES
PAST = PAGE * PAGES
D_FF = 5632
FB = D_FF // P
GROUPS = 4
GF = FB // GROUPS
PLE = 256
CHUNK = 16
NCH = SEQ // CHUNK
CPB = P // CHUNK
EPS = 1e-6
LAM_INIT = 0.8 - 0.6
FINITE = 3e38
SCALE = DK ** -0.5
KC = 8
DOWN_TILES = (6, 5)
GATE_TILES = 6

BLOCK_AT = {"q": 0, "k": 1024, "v": 2048, "f": 4096, "i": 5120, "r": 3072, "g": 6144}
BLOCKS = list(BLOCK_AT)

HEAD_CHUNKS = 2 * len(BLOCKS)
OUT_CHUNKS = 2 * KT
FF_CHUNKS = 4 * GF
DOWN_CHUNKS = 2 * KT
GROUP_CHUNKS = FF_CHUNKS + DOWN_CHUNKS
PLE_CHUNKS = 3 * KT
C_OUT = HEADS * HEAD_CHUNKS
C_RNN = C_OUT + KT
C_FFN = C_OUT + OUT_CHUNKS
C_PLE = C_FFN + GROUPS * GROUP_CHUNKS
C_END = C_PLE + PLE_CHUNKS

ATTENTION = {
    5: ["ssq_q"], 7: ["rot_q"], 9: ["ssq_k"],
    13: ["rot_k", "pages0"], 14: ["pages1", "v_nat"], 15: ["k_nat", "score0"],
    16: ["s_score"], 17: ["score1"], 18: ["w0"], 19: ["s_prob", "score2", "w1"],
    21: ["score3"], 22: ["w2"], 24: ["w3", "s_out"], 25: ["s_turn", "att_out"], 27: ["ssq_a"],
}
RECURRENCE = {
    3: ["i_nat"], 5: ["kh_nat", "intra"], 6: ["upd0"], 8: ["upd1", "rnn0"], 10: ["upd2", "rnn1"],
    12: ["upd3", "rnn2"], 15: ["rnn3"], 16: ["s_upd"], 18: ["s_rnn"], 20: ["ssq_r"],
}
HALVES = 2 * HEAD_CHUNKS
K_PAGES_AT = {True: {10: range(NPG)}, False: {6: range(0, 6), 8: range(6, 11), 10: range(11, NPG)}}
V_PAGES_AT = {18: range(0, 6), 20: range(6, 11), 22: range(11, NPG)}


def tasks_of(attention, recurrence):
    plan = []
    for s in range(HALVES):
        plan.append((RECURRENCE.get(s, []) if recurrence else []) + (ATTENTION.get(s, []) if attention else []))
    return plan


def late_parts(plan, s):
    late = ["late_" + name for name in plan[s - 1] if name.startswith("score")] if s > 0 else []
    return (["late_ssq_r"] if s > 1 and "ssq_r" in plan[s - 2] else []) + late


class Scratch:

    def __init__(self):
        self.base = [0, 0]

    def place(self, names):
        names = list(names) + (["pad"] if len(names) % 2 else [])
        self.at = {n: (i % 2, i // 2) for i, n in enumerate(names)}
        self.per = len(names) // 2
        self.start = list(self.base)
        self.padded = names[-1] == "pad"

    def close(self, times):
        self.base = [b + times * self.per for b in self.start]

    def last(self, it):
        return 1, it * self.per + self.start[1]

    def place_ffn(self):
        self.at = {"c_old": (0, 0), "c_new": (1, 0)}
        self.per = 1
        self.start = list(self.base)
        self.padded = False

    def close_ffn(self):
        self.base = [self.start[0] + GROUPS, self.start[1] + FB]

    def task(self, name, it=0):
        b, i = self.at[name]
        return b, it * self.per + (self.start[b] + i + 1)


ROWS_A = {"norm_mix": 0, "norm_ffn": 16, "norm_ple": 32, "lb0": 48, "lb1": 56, "q": 64, "k": 65, "att": 66, "rnn": 67}
NROWS_A = 68
COL_CW = [NROWS_A, NROWS_A + FB, NROWS_A + 2 * FB, NROWS_A + 3 * FB]
NCOLS = NROWS_A + 4 * FB
FF_STEPS = 4
EARLY_CHUNKS = 4
POOL_TILES = 7
SUM_EARLY = KT - POOL_TILES
EARLY_SPLITS = {KC - 1: 1, KC + 4: 2}

_K = {}
_n = 0
for _name, _w in (("ident", P), ("ones", P), ("eps", 1),
                  ("swap", P), ("ones64", P), ("cos", T), ("sin", T),
                  ("causal", SEQ), ("restart", SEQ), ("chunk_pairs", P), ("chunk_of", CPB),
                  ("pad_q", NS * 16), ("delta8", NS * NS), ("delta_p", NS), ("pairs", NS),
                  ("coef", 2), ("maps", 2)):
    _K[_name] = (_n, _w)
    _n += _w
NCONST = _n
NKEPT = _K["swap"][0]


def constants():
    c = np.zeros((P, NCONST), np.float32)

    def put(name, a):
        at, w = _K[name]
        c[: a.shape[0], at:at + w] = a

    p = np.arange(P)
    put("ident", np.eye(P, dtype=np.float32))
    swap = np.zeros((P, P), np.float32)
    for d in range(P):
        if d % DK < DK // 2:
            swap[d + DK // 2, d] = -1.0
        else:
            swap[d - DK // 2, d] = 1.0
    put("swap", swap)
    put("ones64", (p[:, None] // DK == p[None, :] // DK).astype(np.float32))
    put("ones", np.ones((P, P), np.float32))
    half = DK // 2
    inv = (np.float32(1.0) / np.power(np.float32(10000.0), np.arange(half, dtype=np.float32) * np.float32(2.0 / DK))).astype(np.float32)
    pos = np.concatenate([np.arange(SEQ), np.full(NS, PAST)]).astype(np.float32)
    ang = (inv[p % half][:, None] * pos[None, :]).astype(np.float32)
    put("cos", np.cos(ang).astype(np.float32))
    put("sin", np.sin(ang).astype(np.float32))
    causal = np.zeros((P, SEQ), np.float32)
    causal[:, SEQ - P:] = np.where(p[None, :] <= p[:, None], 0.0, -1e30)
    put("causal", causal)
    put("restart", np.tile((np.arange(SEQ) % CHUNK != 0).astype(np.float32), (P, 1)))
    same = p[:, None] // CHUNK == p[None, :] // CHUNK
    put("chunk_pairs", (same & (p[:, None] <= p[None, :])).astype(np.float32))
    put("chunk_of", (p[:, None] // CHUNK == np.arange(CPB)[None, :]).astype(np.float32))
    pad = np.zeros((P, NS, NS, 2), np.float32)
    for b in range(NS):
        for m in range(2):
            pad[m * DK:(m + 1) * DK, b, b, m] = 1.0
    put("pad_q", pad.reshape(P, -1))
    put("delta8", np.tile(np.eye(NS, dtype=np.float32).reshape(1, -1), (P, 1)))
    put("delta_p", np.eye(NS, dtype=np.float32))
    put("pairs", (np.arange(16)[:, None] // 2 == np.arange(NS)[None, :]).astype(np.float32))
    put("coef", np.stack([np.arange(16) % 2 == 0, -(np.arange(16) % 2.0)], 1).astype(np.float32))
    put("eps", np.full((P, 1), EPS, np.float32))
    put("maps", np.stack([p < DK, p >= DK], 1).astype(np.float32))
    return c


def program(nc, a, o):
    ctx = ExitStack()
    early, heads, late = ExitStack(), ExitStack(), ExitStack()

    def sem(name):
        return ctx.enter_context(nc.semaphore(name))

    def sb(name, shape, dt=F32, into=ctx):
        return into.enter_context(nc.sbuf_tensor(name, shape, dt))

    mix_d = nc.dram_tensor("mix_scratch", [KT, P, T], F32, kind="Internal").ap()
    xt_d = nc.dram_tensor("x_scratch", [KT, P, T], F32, kind="Internal").ap()

    const = sb("const", [P, NKEPT])
    vecs = sb("vecs", [P, NCOLS])
    act_hi = sb("act_hi", [P, KT, T], F32R)
    act_lo = sb("act_lo", [P, KT, T], F32R)
    w_raw = sb("w_raw", [P, 2, KC, P])
    w_hi = sb("w_hi", [P, 2, KC, P], F32R)
    w_lo = sb("w_lo", [P, 2, KC, P], F32R)
    R = sb("R", [P, T])
    sq_sum = sb("sq_sum", [P, T])
    sqx = sb("sqx", [P, 2, T])
    pad_out = sb("pad_out", [32, 1])

    def K(name):
        at, w = _K[name]
        return const[:, at:at + w] if at < NKEPT else tables[:, at - NKEPT:at - NKEPT + w]

    def vec(row, n=1):
        return vecs[:, row:row + n]

    ident = K("ident")

    x_nat = sb("x_nat", [P, 4, D], into=early)
    xs_nat = sb("xs_nat", [NS, D], into=early)
    xT0 = sb("xT0", [P, KT, T], into=early)
    sq_pool = sb("sq_pool", [P, T], into=early)
    rows_a = sb("rows_a", [P, P], into=early)
    rows_b = sb("rows_b", [P, 2, P], into=early)
    early.close()

    def hb(name, shape, dt=F32):
        return sb(name, shape, dt, heads)

    kT = hb("kT", [P, NS, PAST + 1])
    q_map = hb("q_map", [P, 2, SEQ])
    score = hb("score", [P, 2, SEQ])
    wgt = hb("wgt", [P, SEQ])
    wT = hb("wT", [P, 10, P])
    k_pages = hb("k_pages", [P, NPG, P])
    k_nat = hb("k_nat", [P, 5, P])
    v_nat = hb("v_nat", [P, 5, P])
    coef = hb("coef", [16, 1])
    lb = hb("lb", [P, HEADS])
    oml = hb("oml", [P, HEADS])
    lbt = hb("lbt", [P, 3, HEADS])
    gain_a = hb("gain_a", [P, 1])
    z_q = hb("z_q", [P, T])
    z_k = hb("z_k", [P, T])
    z_v = hb("z_v", [P, T])
    sq, rot, zn = sqx[:, 0, :], sqx[:, 1, :], sq_sum
    rr = hb("rr", [P, T])
    q_rot, k_rot = z_q, z_k
    row_max = hb("row_max", [P, 2])
    neg_max = hb("neg_max", [P, 2])
    row_sum = hb("row_sum", [P, 2])
    row_inv = hb("row_inv", [P, 2])
    row_lam = hb("row_lam", [P, 1])
    v_pages = k_pages
    q_pad = hb("q_pad", [P, NS, 16])
    s_p = hb("s_p", [16, PAST + 1])
    s_stat = hb("s_stat", [16, 5])
    w_sum = hb("w_sum", [P, NPG])
    w_pad = hb("w_pad", [P, NPG, NS])
    s_o = hb("s_o", [NS, P])
    v_two = hb("v_two", [P, 16])
    new_w = hb("new_w", [P, NS])
    new_v = hb("new_v", [P, P])
    oT = hb("oT", [P, T])
    mix_a = hb("mix_a", [P, T])
    mix_r = hb("mix_r", [P, T])
    r_o = hb("r_o", [P, T])
    r_g = r_o
    z_f = hb("z_f", [P, T])
    z_i = hb("z_i", [P, T])
    z_r = hb("z_r", [P, T])
    z_g = hb("z_g", [P, T])
    r_k = hb("r_k", [P, T])
    f_s = hb("f_s", [P, NS])
    r_b = hb("r_b", [P, SEQ])
    r_e = hb("r_e", [P, SEQ])
    r_kd = r_b
    r_kh = hb("r_kh", [P, SEQ])
    r_qd = z_r[:, 0:SEQ]
    i_nat = hb("i_nat", [P, 5, P])
    ks_nat = hb("ks_nat", [NS, P])
    kh_nat = hb("kh_nat", [P, 4, P])
    intra = hb("intra", [P, 4, P])
    state = hb("state", [P, 2, CPB, P])
    s_state = hb("s_state", [P, NS, P])
    v_chunks = hb("v_chunks", [P, CPB, P])
    s_iexp = v_chunks[0:NS]
    tables = hb("tables", [P, NCONST - NKEPT])
    lamv = hb("lamv", [P, 4, DK])
    lams = hb("lams", [P, 8])
    lam = hb("lam", [P, 1])
    pages_sb = hb("pages_sb", [1, NPG], I32)
    heads.close()

    def lt(name, shape, dt=F32):
        return sb(name, shape, dt, late)

    xT = lt("xT", [P, KT, T])
    pT_hi = lt("pT_hi", [P, 2, T], F32R)
    pT_lo = lt("pT_lo", [P, 2, T], F32R)
    out_, ffn_, ple_ = ExitStack(), ExitStack(), ExitStack()
    p_nat = sb("p_nat", [P, 5, PLE], into=out_)
    pT = sb("pT", [P, 2, T], into=out_)
    out_.close()
    u_hi = sb("u_hi", [P, GF, T], F32R, ffn_)
    u_lo = sb("u_lo", [P, GF, T], F32R, ffn_)
    ffg = sb("ffg", [P, T + 2], into=ffn_)
    ffc = sb("ffc", [P, T], into=ffn_)
    ffs = sb("ffs", [P, T], into=ffn_)
    ffu = sb("ffu", [P, T], into=ffn_)
    conv_in = sb("conv_in", [16, GF * P], into=ffn_)
    conv_old = sb("conv_old", [P, GF, NS, 2], into=ffn_)
    conv_new = conv_in[0:10]
    ffn_.close()
    gate = sb("gate", [P, T], into=ple_)
    y_t = sb("y_t", [P, 2, T], into=ple_)
    y_nat = sb("y_nat", [P, 2, 5, P], into=ple_)
    ple_.close()
    late.close()

    G = [ctx.enter_context(nc.psum_tensor(f"product{i}", [P, 2, 512], F32)) for i in range(2)]
    M = [ctx.enter_context(nc.psum_tensor(f"scratch{i}", [P, 2, 512], F32)) for i in range(2)]

    w_landed = [sem(f"w_landed{i}") for i in range(2)]
    w_hi_ready, w_lo_ready, w_used = sem("w_hi_ready"), sem("w_lo_ready"), sem("w_used")
    g_free = [sem(f"product{i}_free") for i in range(2)]
    full = [sem(f"scratch{i}_full") for i in range(2)]
    free = [sem(f"scratch{i}_free") for i in range(2)]
    S = {}

    def flag(name):
        if name not in S:
            S[name] = sem(name)
        return S[name]

    def two(ap):
        return ap.rearrange("p (a b) -> p a b", a=2)

    def flat(ap):
        return ap.rearrange("p a b -> p (a b)")

    def m_wide(b):
        return M[b][:, :, 0:TH]

    scratch = Scratch()
    plans = [tasks_of(True, False), tasks_of(True, True), tasks_of(False, True)]
    spans = [(0, 1), (1, HEADS), (HEADS, HEADS + 1)]

    PER_HEAD = [4, 3]
    g_out = [HEADS * 4, HEADS * 3]
    g_rnn = [x + KT // 2 for x in g_out]
    g_ffn = [x + KT // 2 for x in g_rnn]
    g_per_group = GF + KT // 2
    g_ple = [x + GROUPS * g_per_group for x in g_ffn]

    early_names = ["rows_a", "rows_b", "xs"] + [f"x{t}{i}" for t in range(4) for i in range(2)] + ["ssx"]

    def phases(visit):
        scratch.base = [0, 0]
        scratch.place(early_names)
        visit("early", None)
        scratch.close(1)
        for plan, (h0, h1) in zip(plans, spans):
            names = [n for slot in plan for n in slot]
            scratch.place(names)
            visit("heads", (plan, h0, h1))
            scratch.close(h1 - h0)
        scratch.place(["p_turn", "ps_turn", "ss_out"])
        visit("out", None)
        scratch.close(1)
        scratch.place_ffn()
        visit("ffn", None)
        scratch.close_ffn()
        scratch.place(["ss_ffn"])
        visit("mid", None)
        scratch.close(1)
        scratch.place(["pp0", "y0", "pp1", "y1"])
        visit("ple", None)
        scratch.close(KT // 2)

    def evacuated(name, h):
        blk = BLOCKS.index(name)
        g = blk % 2
        return g_free[g], h * PER_HEAD[g] + (blk // 2 + 1)

    def read(name, it):
        b, v = scratch.task(name, it)
        return free[b], v

    block = ctx.enter_context(nc.Block())

    @block.sync
    def _(sp):
        w_in = a["w_in"][0].rearrange("(k p) m -> p k m", p=P)
        w_out = a["w_out"][0].rearrange("(k p) m -> p k m", p=P)
        w_gate = a["w_gate"][0].rearrange("(k p) m -> p k m", p=P)
        w_up = a["w_up"][0].rearrange("(k p) m -> p k m", p=P)
        w_down = a["w_down"][0].rearrange("(k p) m -> p k m", p=P)
        w_pg = a["w_ple_gate"][0].rearrange("(k p) m -> p k m", p=P)
        w_pp = a["w_ple_proj"][0].rearrange("(k p) m -> p k m", p=P)

        def load(c, slot, w, k0, n, col):
            src = w[:, bass.ds(k0, n), bass.ds(col, P)]
            if not isinstance(c, int) or c >= 2:
                sp.wait_ge(w_hi_ready, c - 1)
                sp.wait_ge(w_lo_ready, c - 1)
            sp.dma_start(w_raw[:, slot, 0:n, :], src).then_inc(w_landed[slot], 16)

        def setup():
            sp.dma_start(const[:, :], a["consts"][:, 0:NKEPT]).then_inc(flag("const_in"), 16)
            rows = [("norm_mix", 0, 16), ("norm_ffn", 16, 16), ("norm_ple", 32, 16)]
            for name, r, n in rows:
                sp.dma_start(rows_a[r:r + n, :], a[name][0].rearrange("(b p) -> b p", p=P)).then_inc(flag("rows_in"), 16)
            sp.dma_start(rows_a[48:64, :], a["lower_bounds"].rearrange("r (b p) -> (r b) p", p=P)).then_inc(flag("rows_in"), 16)
            for name, r in (("q_norm", 64), ("k_norm", 65)):
                for m in range(2):
                    sp.dma_start(rows_a[r:r + 1, m * DK:(m + 1) * DK], a[name]).then_inc(flag("rows_in"), 16)
            for name, r in (("att_out_norm", 66), ("rnn_out_norm", 67)):
                sp.dma_start(rows_a[r:r + 1, :], a[name]).then_inc(flag("rows_in"), 16)
            for j in range(4):
                src = a["conv_w"][0, j] if j < 3 else a["conv_b"][0]
                sp.dma_start(rows_b[(j % 2) * FB:(j % 2 + 1) * FB, j // 2, :], src.rearrange("(b p) -> b p", p=P)).then_inc(flag("rows_in"), 16)
            sp.dma_start(xs_nat[:, :], a["x_sample"].rearrange("b t d -> (b t) d")).then_inc(flag("xs_in"), 16)
            for t in range(4):
                for i in range(2):
                    cols = slice(i * (D // 2), (i + 1) * (D // 2))
                    sp.dma_start(x_nat[:, t, cols], a["x_prompt"][0, t * P:(t + 1) * P, cols]).then_inc(flag(f"x_in{t}{i}"), 16)
                if t == 1:
                    load(0, 0, w_in, 0, KC, BLOCK_AT["q"])
            load(1, 1, w_in, KC, KC, BLOCK_AT["q"])
            sp.dma_start(tables[:, :], a["consts"][:, NKEPT:]).then_inc(flag("tables_in"), 16)
            for n, name in enumerate(("lam_q1", "lam_k1", "lam_q2", "lam_k2")):
                sp.dma_start(lamv[:, n, :], a[name].to_broadcast([P, DK])).then_inc(flag("lam_in"), 16)
            sp.dma_start(pages_sb[:, :], a["page_table"].rearrange("b n -> (b n)").rearrange("(o n) -> o n", o=1)).then_inc(flag("pages_in"), 16)
            load(2, 0, w_in, 0, KC, BLOCK_AT["k"])
            load(3, 1, w_in, KC, KC, BLOCK_AT["k"])
            sp.wait_ge(flag("pages_in"), 16)

        def weights(h, s):
            if s % 2 == 0:
                j = s // 2
                name = BLOCKS[j // 2]
                load(h * HEAD_CHUNKS + j, j % 2, w_in, (j % 2) * KC, KC, h * P + BLOCK_AT[name])

        def x_back(k):
            if k % HEADS < HEADS - 1:
                sp.wait_ge(flag("act_lo_ready"), KT + k + 1)
            sp.dma_start(xT[:, k, :], xt_d[k]).then_inc(flag(f"x_back{k}"), 16)

        def mix_back(k):
            sp.dma_start(xT[:, k, :], mix_d[k]).then_inc(flag(f"mix_in{k}"), 16)

        def step(plan, it, h, r, pages):
            attention = any("ssq_q" in x for x in plan)
            recurrence = any("ssq_r" in x for x in plan)
            for s in range(HALVES):
                if attention and (not isinstance(h, int) or s >= 2 * EARLY_CHUNKS):
                    weights(h, s)
                if not attention and s % 2 == 0:
                    j = s // 2
                    if j >= 2:
                        load(C_OUT + j, j % 2, w_out, 0, KC, j * P)
                    if j == 2:
                        for k in range(HEADS - 1):
                            x_back(k)
                    if 4 <= j < 4 + HEADS - 1:
                        x_back(HEADS + j - 4)
                if attention and s == (10 if r is None else 6):
                    if r is None:
                        sp.wait_ge(flag("xT_written"), 16)
                        sp.wait_ge(flag("act_lo_ready"), KT)
                        sp.wait_ge(flag("sq_sum_done"), SUM_EARLY)
                    else:
                        sp.wait_ge(flag("mix_a_done"), h)
                if attention and s in K_PAGES_AT[r is None]:
                    for n in K_PAGES_AT[r is None][s]:
                        sp.dma_start(k_pages[:, n, :], a["cache_k"][0, bass.ds(pages[n], 1), :, bass.ds(h, 1), :].rearrange("g t h d -> (g t) (h d)")).then_inc(flag("k_pages_in"), 16)
                if attention and s == 18:
                    for x in ("pages0", "pages1"):
                        b, v = scratch.task(x, it)
                        sp.wait_ge(full[b], v)
                if attention and s in V_PAGES_AT:
                    for n in V_PAGES_AT[s]:
                        sp.dma_start(v_pages[:, n, :], a["cache_v"][0, bass.ds(pages[n], 1), :, bass.ds(h, 1), :].rearrange("g t h d -> (g t) (h d)")).then_inc(flag("v_pages_in"), 16)
                if recurrence and s == 8:
                    if not attention:
                        sp.wait_ge(flag("mix_a_done"), HEADS)
                    sp.dma_start(s_state[:, :, :], a["state_rnn"][0, :, bass.ds(r, 1), :, :].rearrange("b h k v -> k (b h) v")).then_inc(flag("s_state_in"), 16)

        pages = []

        def visit(what, arg):
            if what == "early":
                setup()
                for n in range(NPG):
                    pages.append(sp.value_load(pages_sb[0:1, n:n + 1], min_val=0, max_val=a["cache_k"].shape[1] - 1))
            elif what == "heads":
                plan, h0, h1 = arg
                if h0 == 0:
                    step(plan, 0, 0, None, pages)
                elif h1 == HEADS:
                    with sp.Fori(h0, h1) as h:
                        step(plan, h - 1, h, h - 1, pages)
                    load(C_OUT, 0, w_out, 0, KC, 0)
                    load(C_OUT + 1, 1, w_out, 0, KC, P)
                    b, v = scratch.task("w3", HEADS - 2)
                    sp.wait_ge(full[b], v)
                    sp.wait_ge(flag("mix_a_out"), (HEADS - 1) * 16)
                    for k in range(HEADS - 1):
                        mix_back(k)
                    b, v = scratch.task("att_out", HEADS - 2)
                    sp.wait_ge(full[b], v)
                    sp.wait_ge(flag("mix_r_out"), (HEADS - 1) * 16)
                    sp.wait_ge(flag("k_nat_out"), HEADS * 32)
                    sp.wait_ge(flag("v_nat_out"), HEADS * 32)
                    for k in range(HEADS, KT - 1):
                        mix_back(k)
                    x_back(HEADS - 1)
                    x_back(KT - 1)
                else:
                    step(plan, 0, HEADS, HEADS - 1, pages)
            elif what == "out":
                for n in range(HALVES // 2, KT):
                    load(C_OUT + n, n % 2, w_out, 0, KC, n * P)
                for n in range(2):
                    load(C_RNN + n, n, w_out, KC, KC, n * P)
                sp.wait_ge(flag("act_lo_ready"), 2 * KT)
                sp.wait_ge(flag("s_state_out"), HEADS * 16)
                sp.wait_ge(flag("state_out"), HEADS * 16)
                sp.dma_start(o["conv_sample"][0, :, 0, :], a["state_ffn_conv"][0, :, 1, :]).then_inc(flag("conv_out"), 16)
                for j in range(4):
                    sp.dma_start(p_nat[:, j, :], a["p_prompt"][0, 0, j * P:(j + 1) * P, :]).then_inc(flag("p_in"), 16)
                sp.dma_start(p_nat[0:NS, 4, :], a["p_sample"][0, :, 0, :]).then_inc(flag("p_in"), 16)
                with sp.Fori(1, KT // 2) as it:
                    for n in range(2):
                        load(it * 2 + (C_RNN + n), n, w_out, KC, KC, it * (2 * P) + n * P)
            elif what == "ffn":
                with sp.Fori(0, GROUPS) as g:
                    def ffn_chunk(f, j):
                        w = w_gate if j < 2 else w_up
                        load(g * GROUP_CHUNKS + f * 4 + (C_FFN + j), j % 2, w, (j % 2) * KC, KC, g * (GF * P) + f * P)

                    ffn_chunk(0, 0)
                    ffn_chunk(0, 1)
                    sp.wait_ge(full[0], scratch.task("c_old", g)[1] - 1)
                    sp.wait_ge(flag("conv_out"), g * 32 + 16)
                    sp.dma_start(conv_in[:, :], a["state_ffn_conv"][0].rearrange("b w f -> (b w) f")[:, bass.ds(g * (GF * P), GF * P)]).then_inc(flag("conv_in"), 16)
                    ffn_chunk(0, 2)
                    ffn_chunk(0, 3)
                    with sp.Fori(1, GF) as f:
                        for j in range(4):
                            ffn_chunk(f, j)
                    with sp.Fori(0, KT // 2) as m:
                        for j in range(4):
                            k0, n = ((0, 6), (6, 5))[j % 2]
                            load(g * GROUP_CHUNKS + m * 4 + (C_FFN + FF_CHUNKS + j), j % 2, w_down, g * GF + k0, n, m * (2 * P) + (j // 2) * P)
            elif what == "ple":
                with sp.Fori(0, KT // 2) as m:
                    for j in range(6):
                        c, col = m * 6 + (C_PLE + j), m * (2 * P) + (j // 3) * P
                        if j % 3 < 2:
                            load(c, j % 2, w_pg, (j % 3) * GATE_TILES, GATE_TILES, col)
                        else:
                            n = KT - 2 * GATE_TILES
                            load(c, j % 2, w_pg, 2 * GATE_TILES, n, col)
                            sp.dma_start(w_raw[:, j % 2, n:GATE_TILES, :], w_pp[:, :, bass.ds(col, P)]).then_inc(w_landed[j % 2], 16)
                sp.wait_ge(flag("y_out0"), KT * 16)
                sp.wait_ge(flag("y_out1"), KT * 16)
                sp.wait_ge(flag("conv_out"), 16 + GROUPS * 2 * 16)

        phases(visit)

    @block.tensor
    def _(pe):
        def split_ready(c):
            pe.wait_ge(w_lo_ready, c + 1)

        def product_free(g, n):
            if not isinstance(n, int) or n > 0:
                pe.wait_ge(g_free[g], n)

        def task(name, it, waits=(), counts=(), reads=()):
            b, v = scratch.task(name, it)
            if not isinstance(v, int) or v >= 2:
                pe.wait_ge(free[b], v - 1)
            others = [scratch.at[x][1] for x in reads if scratch.at[x][0] != b]
            if others:
                last = [x for x in reads if scratch.at[x] == (1 - b, max(others))][0]
                pe.wait_ge(*read(last, it))
            for f, n in waits:
                pe.wait_ge(flag(f), n)
            for sem_, n in counts:
                pe.wait_ge(sem_, n)
            return b

        def turn(out, in_, n):
            if n <= 32:
                return pe.matmul(out, in_, ident[0:n, 0:n], start=True, stop=True)
            return pe.transpose(out, in_, ident[0:n, 0:n])

        def wide(name, it, waits, lhsT, rhs):
            wide_into(task(name, it, waits), lhsT, rhs)

        def wide_into(b, lhsT, rhs):
            for half in range(2):
                mm = pe.matmul(M[b][:, half, 0:TH], lhsT, rhs[:, half * TH:(half + 1) * TH], start=True, stop=True)
            mm.then_inc(full[b], 1)

        def small(name, it, h, r):
            n = None if h is None else h + 1
            m = None if r is None else r + 1
            if name == "ssq_q":
                wide(name, it, [("sq_q", n)], K("ones64"), sq)
            elif name == "rot_q":
                wide(name, it, [("zn_done", h * 2 + 1)], K("swap"), zn)
            elif name == "ssq_k":
                wide(name, it, [("sq_k", n)], K("ones64"), sq)
            elif name == "rot_k":
                wide(name, it, [("zn_done", h * 2 + 2)], K("swap"), zn)
            elif name in ("pages0", "pages1"):
                i = int(name[-1])
                b = task(name, it, [("k_pages_in", h * (NPG * 16) + NPG * 16)])
                for y in range(8):
                    mm = turn(M[b][:, y // 4, (y % 4) * P:(y % 4 + 1) * P], k_pages[:, i * 8 + y, :], P)
                mm.then_inc(full[b], 1)
            elif name in ("v_nat", "k_nat", "i_nat"):
                if name == "v_nat":
                    b = task(name, it, [], [evacuated("v", h)])
                    src = z_v
                elif name == "k_nat":
                    b = task(name, it, [("k_rot_done", n)])
                    src = k_rot
                else:
                    b = task(name, it, [("r_k_done", m)], [evacuated("i", r)])
                    src = z_i
                for j in range(4):
                    turn(M[b][:, 0, j * P:(j + 1) * P], src[:, j * P:(j + 1) * P], P)
                mm = turn(M[b][0:NS, 1, 0:P], src[:, SEQ:T], P)
                if name == "i_nat":
                    mm = turn(M[b][0:NS, 1, P:2 * P], r_k[:, SEQ:T], P)
                mm.then_inc(full[b], 1)
            elif name.startswith("score"):
                i = int(name[-1])
                w = (i + 1) * P
                b = task(name, it, [("q_map_done", n), ("k_rot_done", n)])
                for m_ in range(2):
                    mm = pe.matmul(M[b][:, m_, 0:w], q_map[:, m_, i * P:(i + 1) * P], k_rot[:, 0:w], start=True, stop=True)
                mm.then_inc(full[b], 1)
            elif name == "s_score":
                b = task(name, it, [("q_pad_done", n), ("kT_new_done", n)], (), ["pages0", "pages1"])
                for y in range(NS):
                    mm = pe.matmul(M[b][0:16, 0, 0:PAST + 1], q_pad[:, y, :], kT[:, y, :], start=y == 0, stop=y == NS - 1)
                mm.then_inc(full[b], 1)
            elif name in ("w0", "w1", "w2", "w3"):
                i = int(name[-1])
                b = task(name, it, [("wgt_done", h * 4 + (i + 1))])
                for j in range(i + 1):
                    mm = turn(M[b][:, 0, j * P:(j + 1) * P], wgt[:, j * P:(j + 1) * P], P)
                mm.then_inc(full[b], 1)
            elif name == "s_prob":
                b = task(name, it, [("s_p_done", n), ("v_two_done", n)])
                for y in range(2):
                    turn(M[b][:, 0, y * 16:(y + 1) * 16], s_p[:, y * P:(y + 1) * P], 16)
                turn(M[b][0:16, 1, 0:P], v_two[:, :], P).then_inc(full[b], 1)
            elif name == "s_out":
                b = task(name, it, [("w_pad_done", n), ("new_w_done", n), ("v_pages_in", h * (NPG * 16) + NPG * 16)])
                out = M[b][0:NS, 0, 0:P]
                for y in range(NPG):
                    pe.matmul(out, w_pad[:, y, :], v_pages[:, y, :], start=y == 0, stop=False)
                pe.matmul(out, new_w[:, :], new_v[:, :], start=False, stop=True).then_inc(full[b], 1)
            elif name == "s_turn":
                b = task(name, it, [], (), ["s_out"])
                turn(M[b][:, 0, 0:NS], s_o[:, :], NS).then_inc(full[b], 1)
            elif name == "att_out":
                b = task(name, it, [], (), ["w2", "w3", "v_nat"])
                for i in range(4):
                    for j in range(i + 1):
                        mm = pe.matmul(M[b][:, 0, i * P:(i + 1) * P], v_nat[:, j, :], wT[:, i * (i + 1) // 2 + j, :], start=j == 0, stop=j == i)
                mm.then_inc(full[b], 1)
            elif name == "ssq_a":
                wide(name, it, [("sq_a", n)], K("ones"), sq)
            elif name == "kh_nat":
                b = task(name, it, [("r_kh_done", m)])
                for j in range(4):
                    mm = turn(M[b][:, 0, j * P:(j + 1) * P], r_kh[:, j * P:(j + 1) * P], P)
                mm.then_inc(full[b], 1)
            elif name == "intra":
                b = task(name, it, [("r_kd_done", m), ("r_qd_done", m)])
                for j in range(4):
                    t = slice(j * P, (j + 1) * P)
                    mm = pe.matmul(M[b][:, 0, t], r_kd[:, t], r_qd[:, t], start=True, stop=True)
                mm.then_inc(full[b], 1)
            elif name.startswith("upd"):
                j = int(name[-1])
                b = task(name, it, [("v_chunks_done", r * 4 + (j + 1))], (), ["kh_nat"])
                for y in range(2):
                    mm = pe.matmul(M[b][:, y, :], kh_nat[:, j, :], flat(v_chunks[:, y * 4:(y + 1) * 4, :]), start=True, stop=True)
                mm.then_inc(full[b], 1)
            elif name in ("rnn0", "rnn1", "rnn2", "rnn3"):
                j = int(name[-1])
                b = task(name, it, [("state_done", r * 28 + (j * 7 + 7)), ("intra_done", m)])
                mm = pe.matmul(M[b][:, 0, 0:P], i_nat[:, j, :], intra[:, j, :], start=True, stop=False, skip_group_check=True)
                for c in range(CPB):
                    if j == 0 and c == 0:
                        continue
                    mm = pe.matmul(M[b][:, 0, c * CHUNK:(c + 1) * CHUNK], state[:, j % 2, c, :], r_qd[:, (j * CPB + c) * CHUNK:(j * CPB + c + 1) * CHUNK],
                                   start=False, stop=c == CPB - 1, skip_group_check=True)
                mm.then_inc(full[b], 1)
            elif name == "s_upd":
                b = task(name, it, [("s_iexp_done", m)], (), ["i_nat"])
                for y in range(2):
                    mm = pe.matmul(M[b][:, y, :], ks_nat[:, :], flat(s_iexp[:, y * 4:(y + 1) * 4, :]), start=True, stop=True)
                mm.then_inc(full[b], 1)
            elif name == "s_rnn":
                b = task(name, it, [], (), ["s_upd"])
                for y in range(NS):
                    mm = pe.matmul(M[b][:, 0, y:y + 1], s_state[:, y, :], z_r[:, SEQ + y:SEQ + y + 1], start=True, stop=True)
                mm.then_inc(full[b], 1)
            elif name == "ssq_r":
                wide(name, it, [("sq_r", m)], K("ones"), mix_r)

        def pad(it):
            if scratch.padded:
                b = task("pad", it)
                pe.matmul(M[b][0:32, 0, 0:64], ident[:, 0:32], ident[:, 0:64], start=True, stop=True).then_inc(full[b], 1)

        def step(plan, it, h, r):
            for s in range(HALVES):
                if h is not None:
                    j = s // 2
                    c = h * HEAD_CHUNKS + j
                    blk, g = j // 2, (j // 2) % 2
                    if s % 2 == 0:
                        split_ready(c)
                    if s % 4 == 0:
                        product_free(g, h * PER_HEAD[g] + blk // 2)
                    mm = part(g, j % 2, (s % 2) * 4, (s % 4) * 4, 4, s % 4 == 0, s % 4 == 3, act_hi, act_lo,
                              ("act_lo_ready", (s % 4) * 4 + 1) if r is None and s < 4 else None)
                    if s % 2 == 1:
                        mm.then_inc(w_used, 1)
                if h is None:
                    n = s // 2
                    if s % 2 == 0:
                        split_ready(C_OUT + n)
                        product_free(n % 2, g_out[n % 2] + n // 2)
                    mm = part(n % 2, n % 2, (s % 2) * 4, (s % 2) * 4, 4, s % 2 == 0, s % 2 == 1, act_hi, act_lo,
                              ("act_lo_ready", KT + 1 + (s % 2) * 4) if n == 0 else None)
                    if s % 2 == 1:
                        mm.then_inc(w_used, 1)
                if r is None and s == 4:
                    sum_of_squares(SUM_EARLY)
                    pe.wait_ge(flag("tables_in"), 16)
                for name in plan[s]:
                    small(name, it, h, r)
            pad(it)

        def sum_of_squares(n):
            b, v = sum_task
            pe.wait_ge(free[b], v - 1)
            pe.wait_ge(flag("sq_sum_done"), n)
            wide_into(b, K("ones"), sq_sum)

        def part(g, slot, j0, k0, n, first, last, hi, lo, wait_k=None, wait_last=None):
            return passes(G[g], slot, j0, k0, n, first, last, hi, lo, wait_k, wait_last)

        def passes(out, slot, j0, k0, n, first, last, hi, lo, wait_k=None, wait_last=None):
            mm = None
            for j in range(n):
                if wait_k is not None:
                    pe.wait_ge(flag(wait_k[0]), wait_k[1] + j)
                if wait_last is not None and j == n - 1:
                    pe.wait_ge(flag(wait_last[0]), wait_last[1])
                for which, (w, x) in enumerate(((w_hi, hi), (w_hi, lo), (w_lo, hi))):
                    for half in range(2):
                        t = slice(half * TH, (half + 1) * TH)
                        mm = pe.matmul(out[:, half, 0:TH], w[:, slot, j0 + j, :], x[:, k0 + j, t],
                                       start=first and j == 0 and which == 0,
                                       stop=last and j == n - 1 and which == 2)
            return mm

        def full_product(g, n_free, c, sizes, hi, lo, wait_k=None, slot0=0, k0=0, wait_last=None):
            product_free(g, n_free)
            k = k0
            for j, n in enumerate(sizes):
                split_ready(c + j)
                slot = (slot0 + j) % 2
                mm = part(g, slot, 0, k, n, j == 0, j == len(sizes) - 1, hi, lo,
                          None if wait_k is None else (wait_k[0], wait_k[1] + k),
                          wait_last if j == len(sizes) - 1 else None)
                mm.then_inc(w_used, 1)
                k += n

        sum_task = None

        def visit(what, arg):
            nonlocal sum_task
            if what == "early":
                pe.wait_ge(flag("const_in"), 16)
                pe.wait_ge(flag("rows_in"), 14 * 16)
                b = task("rows_a", 0)
                turn(M[b][:, 0, 0:NROWS_A], rows_a[0:NROWS_A, :], NROWS_A).then_inc(full[b], 1)
                b = task("rows_b", 0)
                for j in range(2):
                    mm = turn(M[b][:, 0, j * 2 * FB:(j + 1) * 2 * FB], rows_b[0:2 * FB, j, :], 2 * FB)
                mm.then_inc(full[b], 1)
                pe.wait_ge(flag("xs_in"), 16)
                b = task("xs", 0)
                for y in range(16):
                    mm = turn(M[b][:, 0, y * NS:(y + 1) * NS], xs_nat[:, y * P:(y + 1) * P], NS)
                mm.then_inc(full[b], 1)
                for t in range(4):
                    for i in range(2):
                        pe.wait_ge(flag(f"x_in{t}{i}"), 16)
                        b = task(f"x{t}{i}", 0)
                        for y in range(8):
                            mm = turn(M[b][:, y // 4, (y % 4) * P:(y % 4 + 1) * P], x_nat[:, t, (i * 8 + y) * P:(i * 8 + y + 1) * P], P)
                        mm.then_inc(full[b], 1)
                sum_task = scratch.task("ssx", 0)
            elif what == "heads":
                plan, h0, h1 = arg
                if h0 == 0:
                    step(plan, 0, 0, None)
                elif h1 == HEADS:
                    with pe.Fori(h0, h1) as h:
                        step(plan, h - 1, h, h - 1)
                else:
                    step(plan, 0, None, HEADS - 1)
            elif what == "out":
                for n in range(HALVES // 2, KT):
                    full_product(n % 2, g_out[n % 2] + n // 2, C_OUT + n, (KC,), act_hi, act_lo, slot0=n % 2)

                def out_product(it, x, wait_k=None):
                    full_product(x, it + g_rnn[x], it * 2 + (C_RNN + x), (KC,), act_hi, act_lo, wait_k, x, KC)
                out_product(0, 0, ("act_lo_ready", KT + 1))
                out_product(0, 1)
                with pe.Fori(1, KT // 4) as it:
                    for x in range(2):
                        out_product(it, x)
                b = task("p_turn", 0, [("p_in", 80)])
                for half in range(2):
                    for j in range(4):
                        mm = turn(M[b][:, half, j * P:(j + 1) * P], p_nat[:, j, half * P:(half + 1) * P], P)
                mm.then_inc(full[b], 1)
                b = task("ps_turn", 0)
                for half in range(2):
                    mm = turn(M[b][:, 0, half * NS:(half + 1) * NS], p_nat[0:NS, 4, half * P:(half + 1) * P], NS)
                mm.then_inc(full[b], 1)
                with pe.Fori(KT // 4, KT // 2) as it:
                    for x in range(2):
                        out_product(it, x)
                wide("ss_out", 0, [("sq_sum_done", SUM_EARLY + KT)], K("ones"), sq_sum)
                pad(0)
            elif what == "ffn":
                with pe.Fori(0, GROUPS) as g:
                    def ff_block(f, first):
                        n = g * GF + f
                        for x in range(2):
                            full_product(x, g * g_per_group + f + g_ffn[x], g * GROUP_CHUNKS + f * 4 + (C_FFN + 2 * x), (KC, KC), act_hi, act_lo,
                                         ("act_lo_ready", 2 * KT + 1) if first and x == 0 else None)
                            if first and x == 0:
                                b = task("c_old", g, [("conv_in", g * 16 + 16)])
                                for i in range(GF):
                                    mm = turn(M[b][:, 0, i * 16:(i + 1) * 16], conv_in[:, i * P:(i + 1) * P], 16)
                                mm.then_inc(full[b], 1)
                        b = task("c_new", n, [], [(g_free[0], g * g_per_group + f + (g_ffn[0] + 1))])
                        turn(M[b][0:10, 0, 0:P], ffg[:, SEQ:SEQ + 10], P).then_inc(full[b], 1)

                    ff_block(0, True)
                    with pe.Fori(1, GF) as f:
                        ff_block(f, False)
                    with pe.Fori(0, KT // 2) as m:
                        pe.wait_ge(flag("u_done"), g * GF + (GF - 1))
                        for x in range(2):
                            full_product(x, g * g_per_group + m + (g_ffn[x] + GF), g * GROUP_CHUNKS + m * 4 + (C_FFN + FF_CHUNKS + 2 * x), DOWN_TILES, u_hi, u_lo,
                                         wait_last=("u_done", g * GF + GF))
            elif what == "mid":
                sum_task = scratch.task("ss_ffn", 0)
                pad(0)
            elif what == "ple":
                def y_turn(x, m):
                    b = task(f"y{x}", m, [("y_done", m * 2 + (x + 1))])
                    for j in range(4):
                        turn(M[b][:, 0, j * P:(j + 1) * P], y_t[:, x, j * P:(j + 1) * P], P)
                    turn(M[b][0:NS, 1, 0:P], y_t[:, x, SEQ:T], P).then_inc(full[b], 1)

                def ple(m, x, before):
                    n = KT - 2 * GATE_TILES
                    c = m * 6 + (C_PLE + 3 * x)
                    product_free(x, m + g_ple[x])
                    for j in range(3):
                        slot = (3 * x + j) % 2
                        k = j * GATE_TILES
                        split_ready(c + j)
                        if j == 2:
                            b = task(f"pp{x}", m)
                            passes(M[b], slot, n, 0, GATE_TILES - n, True, True, pT_hi, pT_lo).then_inc(full[b], 1)
                        part(x, slot, 0, k, GATE_TILES if j < 2 else n, j == 0, j == 2, act_hi, act_lo,
                             ("act_lo_ready", 3 * KT + 1 + k) if before is None else None).then_inc(w_used, 1)
                        if j == 0 and before is None:
                            sum_of_squares(SUM_EARLY + (1 + GROUPS) * KT)
                        if j == 0 and before is not None:
                            y_turn(*before)

                ple(0, 0, None)
                ple(0, 1, (0, 0))
                with pe.Fori(1, KT // 2) as m:
                    ple(m, 0, (1, m - 1))
                    ple(m, 1, (0, m))
                y_turn(1, KT // 2 - 1)

        phases(visit)

    CP = (PAST + 1)

    def pages_view(b):
        return M[b][:, :, :].rearrange("p a (y t) -> p (a y) t", y=2)

    def column(tile, k, n=1):
        return tile[:, bass.ds(k, n), :].rearrange("p a b -> p (a b)")

    @block.scalar
    def _(act):
        def split(c, c2, slot, n=KC):
            act.wait_ge(w_landed[slot], c2 * 16 + 16)
            if not isinstance(c, int) or c >= 2:
                act.wait_ge(w_used, c - 1)
            act.activation(w_hi[:, slot, 0:n, :], w_raw[:, slot, 0:n, :], ACT.Copy).then_inc(w_hi_ready, 1)

        def take(name, it, waits=()):
            b, v = scratch.task(name, it)
            act.wait_ge(full[b], v)
            for f, n in waits:
                act.wait_ge(flag(f), n)
            return b

        def func(out, in_, f, **kw):
            return act.activation(out, in_, f, **kw)

        def small(name, it, h, r):
            n = None if h is None else h + 1
            m = None if r is None else r + 1
            if name in ("ssq_q", "ssq_k", "ssq_a", "ssq_r"):
                if name == "ssq_a":
                    b, v = scratch.last(it)
                    act.wait_ge(full[b], v)
                else:
                    b, v = take(name, it), scratch.task(name, it)[1]
                count = DK if name in ("ssq_q", "ssq_k") else P
                if name == "ssq_k":
                    act.wait_ge(flag("zn_done"), h * 2 + 1)
                elif name == "ssq_r":
                    if h is not None:
                        act.wait_ge(flag("zn_done"), h * 2 + 2)
                elif name == "ssq_a":
                    act.wait_ge(*evacuated("r", h))
                elif name == "ssq_q":
                    if h is not None and not isinstance(h, int):
                        act.wait_ge(flag("mix_a_done"), h)
                ln = func(two(rr[:, :]), m_wide(b), ACT.Ln, scale=1.0 / count, bias=K("eps"))
                ln.then_inc(free[b], 1)
                act.wait_ge(free[b], v)
                sig = {"ssq_q": "rr_q", "ssq_k": "rr_k", "ssq_a": "rr_a", "ssq_r": "rr_r"}[name]
                func(rr[:, :], rr[:, :], ACT.Exp, scale=-0.5).then_inc(flag(sig), 1)
            elif name in ("pages0", "pages1"):
                i = int(name[-1])
                b = take(name, it)
                func(kT[:, i * 4:(i + 1) * 4, 0:PAST], pages_view(b), ACT.Copy).then_inc(free[b], 1)
            elif name in ("k_nat", "v_nat"):
                dst, outs = (k_nat, ("k_prompt", "k_sample")) if name == "k_nat" else (v_nat, ("v_prompt", "v_sample"))
                b = take(name, it)
                if not isinstance(h, int):
                    act.wait_ge(flag(f"{name}_out"), h * 32)
                act.activation(dst[:, 0:4, :], M[b][:, 0, :].rearrange("p (j d) -> p j d", j=4), ACT.Copy)
                act.activation(dst[0:NS, 4, :], M[b][0:NS, 1, 0:P], ACT.Copy).then_inc(free[b], 1)
                act.wait_ge(free[b], scratch.task(name, it)[1])
                pr = o[outs[0]][0, 0].rearrange("g t h d -> t g h d")[:, :, bass.ds(h, 1), :].rearrange("t g h d -> t g (h d)")
                act.dma_start(pr, dst[:, 0:4, :]).then_inc(flag(f"{name}_out"), 16)
                sa = o[outs[1]][0, :, 0, bass.ds(h, 1), :].rearrange("b h d -> b (h d)")
                act.dma_start(sa, dst[0:NS, 4, :]).then_inc(flag(f"{name}_out"), 16)
            elif name.startswith("score"):
                i = int(name[-1])
                w = (i + 1) * P
                act.wait_ge(flag("neg_max_done"), h * 4 + (i + 1))
                for m_ in range(2):
                    e = func(score[:, m_, 0:w], score[:, m_, 0:w], ACT.Exp, scale=SCALE, bias=neg_max[:, m_:m_ + 1],
                             accum_out=row_sum[:, m_:m_ + 1])
                e.then_inc(flag("exp_done"), 1)
            elif name.startswith("late_score"):
                i = int(name[-1])
                w = (i + 1) * P
                act.wait_ge(flag("row_lam_done"), h * 4 + (i + 1))
                func(score[:, 1, 0:w], score[:, 1, 0:w], ACT.Copy, scale=row_lam[:, 0:1]).then_inc(flag("second_done"), 1)
            elif name == "s_score":
                b = take(name, it, [("s_max_done", n)])
                func(s_p[:, :], M[b][0:16, 0, 0:CP], ACT.Exp, scale=SCALE, bias=s_stat[:, 1:2],
                     accum_out=s_stat[:, 2:3]).then_inc(free[b], 1)
            elif name in ("w0", "w1", "w2", "w3"):
                i = int(name[-1])
                b = take(name, it)
                func(wT[:, i * (i + 1) // 2:(i + 1) * (i + 2) // 2, :], M[b][:, 0, 0:(i + 1) * P].rearrange("p (j q) -> p j q", j=i + 1), ACT.Copy).then_inc(free[b], 1)
            elif name == "s_out":
                b = take(name, it)
                func(s_o[:, :], M[b][0:NS, 0, 0:P], ACT.Copy).then_inc(free[b], 1)
            elif name == "s_turn":
                b = take(name, it)
                func(oT[:, SEQ:T], M[b][:, 0, 0:NS], ACT.Copy).then_inc(free[b], 1)
            elif name == "att_out":
                b = take(name, it)
                func(oT[:, 0:SEQ], M[b][:, 0, :], ACT.Copy).then_inc(free[b], 1)
                act.wait_ge(free[b], scratch.task(name, it)[1])
                sb_, sv = scratch.task("s_turn", it)
                act.wait_ge(free[sb_], sv)
                func(sq[:, :], oT[:, :], ACT.Square).then_inc(flag("sq_a"), 1)
            elif name == "i_nat":
                b = take(name, it)
                func(i_nat[:, 0:4, :], M[b][:, 0, :].rearrange("p (j d) -> p j d", j=4), ACT.Copy).then_inc(flag("i_nat_done"), 1)
                func(i_nat[0:NS, 4, :], M[b][0:NS, 1, 0:P], ACT.Copy)
                func(ks_nat[:, :], M[b][0:NS, 1, P:2 * P], ACT.Copy).then_inc(free[b], 1)
            elif name == "kh_nat":
                b = take(name, it)
                func(kh_nat[:, :, :], M[b][:, 0, :].rearrange("p (j d) -> p j d", j=4), ACT.Copy).then_inc(free[b], 1)
            elif name in ("rnn0", "rnn1", "rnn2", "rnn3"):
                j = int(name[-1])
                b = take(name, it)
                func(r_o[:, j * P:(j + 1) * P], M[b][:, 0, 0:P], ACT.Copy).then_inc(free[b], 1)
            elif name == "s_rnn":
                b = take(name, it)
                func(r_o[:, SEQ:T], M[b][:, 0, 0:NS], ACT.Copy).then_inc(free[b], 1)
                act.wait_ge(free[b], scratch.task(name, it)[1])
                b3, v3 = scratch.task("rnn3", it)
                act.wait_ge(free[b3], v3)
                act.wait_ge(flag("s_state_out"), r * 16 + 16)
                func(mix_r[:, :], r_o[:, :], ACT.Square).then_inc(flag("sq_r"), 1)

        def write_mix(name, h, tile, row):
            act.wait_ge(flag(f"{name}_done"), h + 1)
            act.dma_start(mix_d[bass.ds(row, 1), :, :].rearrange("k p t -> p (k t)"), tile[:, :]).then_inc(flag(f"{name}_out"), 16)

        def mixed(k, src):
            func(act_hi[:, k, :], src, ACT.Copy).then_inc(flag("act_hi_ready"), 1)

        def mixed_back(k):
            act.wait_ge(flag(f"mix_in{k}"), 16)
            mixed(k, xT[:, k, :])

        def step(plan, it, h, r):
            for s in range(HALVES):
                if h is None and s == 0:
                    act.wait_ge(w_used, C_OUT)
                    for k in range(4):
                        mixed_back(k)
                if s % 2 == 0 and (r is not None or s >= 2 * EARLY_CHUNKS - 2):
                    j = s // 2 + 1
                    split((HEADS if h is None else h) * HEAD_CHUNKS + j, (HEADS if h is None else h) * len(BLOCKS) + j // 2, j % 2)
                if r is not None and s == 0:
                    small("ssq_a", it, r, None)
                for name in late_parts(plan, s):
                    small(name, it, h, r)
                if h is None and s == 0:
                    for k in range(4, HEADS - 1):
                        mixed_back(k)
                    act.wait_ge(flag("mix_a_done"), HEADS)
                    mixed(HEADS - 1, mix_a[:, :])
                if h is None and s % 2 == 0 and 2 <= s < 2 * HEADS:
                    mixed_back(HEADS + s // 2 - 1)
                if h is None and s == 24:
                    act.wait_ge(flag("mix_r_done"), HEADS)
                    mixed(KT - 1, mix_r[:, :])
                if r is not None and s == 0:
                    act.wait_ge(*evacuated("f", r))
                    func(r_k[:, :], z_f[:, :], ACT.Sigmoid, scale=-1.0)
                    func(z_f[:, :], z_f[:, :], ACT.Sigmoid).then_inc(flag("sig_f"), 1)
                    act.wait_ge(*evacuated("g", r))
                    func(r_g[:, :], z_g[:, :], ACT.Sigmoid).then_inc(flag("sig_g"), 1)
                    act.wait_ge(flag("f_done"), r + 1)
                    func(r_kh[:, :], z_f[:, 0:SEQ], ACT.Ln).then_inc(flag("log_f"), 1)
                if r is not None and s == 2:
                    act.wait_ge(flag("scan_done"), r + 1)
                    func(r_e[:, :], r_b[:, :], ACT.Exp).then_inc(flag("exp_b"), 1)
                    act.wait_ge(flag("b_left"), r + 1)
                    func(r_kd[:, :], r_b[:, :], ACT.Exp, scale=-1.0).then_inc(flag("exp_nb"), 1)
                    func(r_kh[:, :], r_kh[:, :], ACT.Exp).then_inc(flag("exp_left"), 1)
                if h is not None and s == 4:
                    act.wait_ge(*evacuated("q", h))
                    func(sq[:, :], z_q[:, :], ACT.Square).then_inc(flag("sq_q"), 1)
                if h is not None and s == 8:
                    act.wait_ge(*evacuated("k", h))
                    func(sq[:, :], z_k[:, :], ACT.Square).then_inc(flag("sq_k"), 1)
                for name in plan[s]:
                    if name != "ssq_a":
                        small(name, it, h, r)
                if h is not None and s == 8:
                    act.wait_ge(flag("q_rot_done"), h + 1)
                    for m_ in range(2):
                        e = func(q_map[:, m_, :], q_rot[:, 0:SEQ], ACT.Copy, scale=K("maps")[:, m_:m_ + 1])
                    e.then_inc(flag("q_map_done"), 1)
                if r is not None and s == 13:
                    act.wait_ge(*read("upd3", it))
                    act.dma_start(o["rnn_prompt"][0, 0, bass.ds(r, 1), :, :].rearrange("h k v -> k (h v)"), state[:, 0, 0, :]).then_inc(flag("state_out"), 16)
                if r is not None and s == 17:
                    act.wait_ge(*read("s_upd", it))
                    act.dma_start(o["rnn_sample"][0, :, bass.ds(r, 1), :, :].rearrange("b h k v -> k (b h) v"), s_state[:, :, :]).then_inc(flag("s_state_out"), 16)
                if r is not None and s == 23 and h is not None:
                    write_mix("mix_r", r, mix_r, r + HEADS)
                if r is not None and s == 3 and h is not None:
                    write_mix("mix_a", r, mix_a, r)
            if r is not None and h is not None:
                act.wait_ge(flag("mix_a_out"), r * 16 + 16)
                act.wait_ge(flag("mix_r_out"), r * 16 + 16)

        def operand(k, src, gain):
            func(act_hi[:, k, :], src, ACT.Copy, scale=gain).then_inc(flag("act_hi_ready"), 1)

        def squares(n, slot, src):
            if not isinstance(n, int) or n >= 2:
                act.wait_ge(flag("sq_sum_done"), n - 1)
            func(sqx[:, slot, :], src, ACT.Square).then_inc(flag("squares"), 1)

        def norm(name):
            b = take(name, 0)
            func(two(R[:, :]), m_wide(b), ACT.Ln, scale=1.0 / D, bias=K("eps")).then_inc(free[b], 1)
            act.wait_ge(free[b], scratch.task(name, 0)[1])
            func(R[:, :], R[:, :], ACT.Exp, scale=-0.5).then_inc(flag("R_ready"), 1)

        def write_x(t0, t1, *tasks):
            for name in tasks:
                act.wait_ge(*read(name, 0))
            act.dma_start(xt_d.rearrange("k p t -> p k t")[:, :, t0:t1], xT0[:, :, t0:t1]).then_inc(flag("xT_written"), 16)

        def visit(what, arg):
            if what == "early":
                b = take("xs", 0)
                func(xT0[:, :, SEQ:T], M[b][:, 0, 0:KT * NS].rearrange("p (y c) -> p y c", y=KT), ACT.Copy).then_inc(free[b], 1)
                for t in range(4):
                    b = take(f"x{t}0", 0)
                    func(xT0[:, 0:8, t * P:(t + 1) * P], M[b][:, :, :].rearrange("p a (y c) -> p (a y) c", y=4), ACT.Copy).then_inc(free[b], 1)
                    if t == 2:
                        split(0, 0, 0)
                write_x(0, T, "xs", "x30", "x31")
                act.wait_ge(*read("rows_a", 0))
                act.wait_ge(*read("rows_b", 0))
                for k in range(KT):
                    operand(k, xT0[:, k, :], vec(ROWS_A["norm_mix"] + k))
                    if k in EARLY_SPLITS:
                        c = EARLY_SPLITS[k]
                        split(c, c // 2, c % 2)
                for k in range(SUM_EARLY):
                    squares(k, k % 2, xT0[:, k, :])
                    if k == KT // 2 - 1:
                        split(3, 1, 1)
                b = take("ssx", 0)
                func(two(R[:, :]), m_wide(b), ACT.Ln, scale=1.0 / D, bias=K("eps")).then_inc(free[b], 1)
                act.wait_ge(free[b], scratch.task("ssx", 0)[1])
                func(R[:, :], R[:, :], ACT.Exp, scale=-0.5).then_inc(flag("R_ready"), 1)
                act.wait_ge(flag("tables_in"), 16)
                act.wait_ge(flag("setup_a"), 4)
                func(lams[:, 2:4], lams[:, 0:2], ACT.Exp).then_inc(flag("setup_e"), 1)
                func(lbt[:, 0:2, :], lbt[:, 0:2, :], ACT.Exp).then_inc(flag("setup_e"), 1)
            elif what == "heads":
                plan, h0, h1 = arg
                if h0 == 0:
                    step(plan, 0, 0, None)
                elif h1 == HEADS:
                    with act.Fori(h0, h1) as h:
                        step(plan, h - 1, h, h - 1)
                else:
                    step(plan, 0, None, HEADS - 1)
            elif what == "out":
                for n in range(HALVES // 2 + 1, KT + 2):
                    split(C_OUT + n, (C_OUT + n) // 2, n % 2)

                def out_product(it, x):
                    split(it * 2 + (C_RNN + x + 2), it + (C_RNN // 2 + 1), x)
                    act.wait_ge(g_free[x], it + (g_rnn[x] + 1))
                    squares(it * 2 + (SUM_EARLY + x), x, column(xT, it * 2 + x))
                with act.Fori(0, KT // 4) as it:
                    for x in range(2):
                        out_product(it, x)
                b = take("p_turn", 0)
                func(pT[:, :, 0:SEQ], M[b][:, :, :], ACT.Copy).then_inc(free[b], 1)
                b = take("ps_turn", 0)
                func(pT[:, :, SEQ:T], M[b][:, 0, 0:2 * NS].rearrange("p (a c) -> p a c", a=2), ACT.Copy).then_inc(free[b], 1)
                for nm in ("p_turn", "ps_turn"):
                    b, v = scratch.task(nm, 0)
                    act.wait_ge(free[b], v)
                func(pT_hi[:, :, :], pT[:, :, :], ACT.Copy).then_inc(flag("pT_hi_done"), 1)
                with act.Fori(KT // 4, KT // 2) as it:
                    for x in range(2):
                        out_product(it, x)
                for k in range(KT):
                    act.wait_ge(w_used, C_FFN)
                    if k >= KT - 2:
                        act.wait_ge(g_free[k % 2], g_ffn[k % 2])
                    operand(k, xT[:, k, :], vec(ROWS_A["norm_ffn"] + k))
                norm("ss_out")
            elif what == "ffn":
                with act.Fori(0, GROUPS) as g:
                    def ff_block(f, first):
                        n = g * GF + f
                        cb, c2 = C_FFN, C_FFN // 2

                        def two_chunks(x):
                            for j in (2 * x + 2, 2 * x + 3):
                                split(g * GROUP_CHUNKS + f * 4 + (cb + j), g * (GROUP_CHUNKS // 2) + f * 2 + (c2 + j // 2), j % 2)
                        two_chunks(0)
                        if first:
                            b = take("c_old", g)
                            func(conv_old[:, :, :, :].rearrange("p f b w -> p (f b w)"), M[b][:, 0, 0:GF * 16], ACT.Copy).then_inc(free[b], 1)
                        act.wait_ge(flag("ffc_done"), n + 1)
                        func(ffs[:, :], ffc[:, :], ACT.Silu).then_inc(flag("silu_done"), 1)
                        two_chunks(1)
                        act.wait_ge(flag("ffu_done"), n + 1)
                        func(column(u_hi, f), ffu[:, :], ACT.Copy).then_inc(flag("u_hi_done"), 1)
                        b = take("c_new", n)
                        act.wait_ge(flag("conv_out"), g * 32 + 16)
                        func(conv_new[:, bass.ds(f * P, P)], M[b][0:10, 0, 0:P], ACT.Copy).then_inc(free[b], 1)

                    ff_block(0, True)
                    with act.Fori(1, GF) as f:
                        ff_block(f, False)
                    act.wait_ge(free[1], scratch.task("c_new", g * GF)[1] + (GF - 1))
                    cols = bass.ds(g * (GF * P), GF * P)
                    act.dma_start(o["conv_prompt"][0, 0, :, cols], conv_new[0:2, :]).then_inc(flag("conv_out"), 16)
                    act.dma_start(o["conv_sample"][0, :, 1, cols], conv_new[2:10, :]).then_inc(flag("conv_out"), 16)
                    with act.Fori(0, KT // 2) as m:
                        for x in range(2):
                            for j in (2 * x + 2, 2 * x + 3):
                                split(g * GROUP_CHUNKS + m * 4 + (C_FFN + FF_CHUNKS + j), g * (GROUP_CHUNKS // 2) + m * 2 + ((C_FFN + FF_CHUNKS) // 2 + j // 2), j % 2)
                            act.wait_ge(g_free[x], g * g_per_group + m + (g_ffn[x] + GF + 1))
                            squares(g * KT + m * 2 + (SUM_EARLY + KT + x), x, column(xT, m * 2 + x))
            elif what == "mid":
                for k in range(KT):
                    act.wait_ge(w_used, C_PLE)
                    if k >= KT - 2:
                        act.wait_ge(g_free[k % 2], g_ple[k % 2])
                    operand(k, xT[:, k, :], vec(ROWS_A["norm_ple"] + k))
                norm("ss_ffn")
            elif what == "ple":
                def sp_(m, j):
                    c2 = (0, 0, 2, 1, 3, 3)[j % 6] + 4 * (j // 6)
                    split(m * 6 + (C_PLE + j), m * 4 + (C_PLE // 2 + c2), j % 2, GATE_TILES)

                def y_out(x, m):
                    n = m * 2 + x
                    b = take(f"y{x}", m)
                    if not isinstance(m, int) or m > 0:
                        act.wait_ge(flag(f"y_out{x}"), m * 32)
                    func(y_nat[:, x, 0:4, :], M[b][:, 0, :].rearrange("p (j d) -> p j d", j=4), ACT.Copy)
                    func(y_nat[0:NS, x, 4, :], M[b][0:NS, 1, 0:P], ACT.Copy).then_inc(free[b], 1)
                    act.wait_ge(free[b], scratch.task(f"y{x}", m)[1])
                    cols = bass.ds(n * P, P)
                    act.dma_start(o["y_prompt"][0].rearrange("(j p) d -> p j d", p=P)[:, :, cols], y_nat[:, x, 0:4, :]).then_inc(flag(f"y_out{x}"), 16)
                    act.dma_start(o["y_sample"][:, 0, cols], y_nat[0:NS, x, 4, :]).then_inc(flag(f"y_out{x}"), 16)

                def ple(m, x, before, last=False):
                    sp_(m, 3 * x + 2)
                    if before is not None:
                        y_out(*before)
                    if not last:
                        sp_(m, 3 * x + 3)
                        sp_(m, 3 * x + 4)
                    act.wait_ge(g_free[x], m + (g_ple[x] + 1))
                    func(gate[:, :], gate[:, :], ACT.Sigmoid).then_inc(flag("gate_done"), 1)

                ple(0, 0, None)
                ple(0, 1, (0, 0))
                with act.Fori(1, KT // 2 - 1) as m:
                    ple(m, 0, (1, m - 1))
                    ple(m, 1, (0, m))
                m = KT // 2 - 1
                ple(m, 0, (1, m - 1))
                ple(m, 1, (0, m), last=True)
                y_out(1, m)

        phases(visit)

    @block.vector
    def _(dve):
        def low(c, slot, n=KC):
            dve.wait_ge(w_hi_ready, c + 1)
            dve.tensor_tensor(flat(w_lo[:, slot, 0:n, :]), flat(w_raw[:, slot, 0:n, :]), flat(w_hi[:, slot, 0:n, :]).bitcast(F32),
                              ALU.subtract).then_inc(w_lo_ready, 1)

        def take(name, it, waits=()):
            b, v = scratch.task(name, it)
            dve.wait_ge(full[b], v)
            for f, n in waits:
                dve.wait_ge(flag(f), n)
            return b

        def evacuate(name, h, z):
            blk = BLOCKS.index(name)
            dve.wait_ge(w_used, h * HEAD_CHUNKS + 2 * blk + 2)
            dve.tensor_tensor(two(z[:, :]), G[blk % 2][:, :, 0:TH], two(R[:, :]), ALU.mult).then_inc(g_free[blk % 2], 1)

        def small(name, it, h, r):
            n = None if h is None else h + 1
            m = None if r is None else r + 1
            if name in ("ssq_q", "ssq_k"):
                z, gain, i = (z_q, ROWS_A["q"], 1) if name == "ssq_q" else (z_k, ROWS_A["k"], 2)
                dve.wait_ge(flag("rr_q" if i == 1 else "rr_k"), n)
                dve.scalar_tensor_tensor(zn[:, :], z[:, :], vec(gain), rr[:, :], ALU.mult, ALU.mult).then_inc(flag("zn_done"), 1)
                dve.wait_ge(flag("zn_done"), h * 2 + i)
                dve.tensor_tensor(z[:, :], zn[:, :], K("cos"), ALU.mult).then_inc(flag("cos_done"), 1)
            elif name in ("rot_q", "rot_k"):
                z, dst, i, sig = (z_q, q_rot, 1, "q_rot_done") if name == "rot_q" else (z_k, k_rot, 2, "k_rot_done")
                b = take(name, it)
                dve.tensor_tensor(two(rot[:, :]), m_wide(b), two(K("sin")), ALU.mult).then_inc(free[b], 1)
                dve.wait_ge(free[b], scratch.task(name, it)[1])
                dve.wait_ge(flag("cos_done"), h * 2 + i)
                dve.tensor_tensor(dst[:, :], z[:, :], rot[:, :], ALU.add).then_inc(flag(sig), 1)
                dve.wait_ge(flag(sig), n)
                if name == "rot_q":
                    dve.tensor_tensor(q_pad[:, :, :], q_rot[:, SEQ:T].unsqueeze(2).broadcast_to([P, NS, 16]),
                                      K("pad_q").rearrange("p (b c) -> p b c", b=NS), ALU.mult).then_inc(flag("q_pad_done"), 1)
                else:
                    dve.tensor_copy(kT[:, :, PAST:PAST + 1].rearrange("p b o -> p (b o)"), k_rot[:, SEQ:T]).then_inc(flag("kT_new_done"), 1)
            elif name == "v_nat":
                dve.wait_ge(*evacuated("v", h))
                dve.tensor_copy(v_two[:, :].rearrange("p (b w) -> p b w", w=2),
                                z_v[:, SEQ:T].unsqueeze(2).broadcast_to([P, NS, 2])).then_inc(flag("v_two_done"), 1)
            elif name.startswith("score"):
                i = int(name[-1])
                w = (i + 1) * P
                c = h * 4 + (i + 1)
                b = take(name, it)
                if i > 0 or not isinstance(h, int):
                    dve.wait_ge(flag("wgt_done"), c - 1)
                dve.memset(neg_max[:, :], 0.0)
                for m_ in range(2):
                    t = dve.tensor_tensor_reduce(score[:, m_, 0:w], M[b][:, m_, 0:w], K("causal")[:, SEQ - w:SEQ], 1.0, -3e38,
                                                 ALU.add, ALU.max, row_max[:, m_:m_ + 1])
                t.then_inc(free[b], 1)
                dve.wait_ge(free[b], scratch.task(name, it)[1])
                dve.tensor_scalar(neg_max[:, :], row_max[:, :], -SCALE, None, ALU.mult).then_inc(flag("neg_max_done"), 1)
            elif name.startswith("late_score"):
                i = int(name[-1])
                w = (i + 1) * P
                c = h * 4 + (i + 1)
                dve.wait_ge(flag("exp_done"), c)
                dve.reciprocal(row_inv[:, :], row_sum[:, :]).then_inc(flag("row_inv_done"), 1)
                dve.wait_ge(flag("row_inv_done"), c)
                dve.tensor_tensor(row_lam[:, :], row_inv[:, 1:2], lam[:, :], ALU.mult).then_inc(flag("row_lam_done"), 1)
                dve.wait_ge(flag("second_done"), c)
                if i > 0:
                    b2, v2 = scratch.task(f"w{i - 1}", it)
                    dve.wait_ge(full[b2], v2)
                dve.scalar_tensor_tensor(wgt[:, 0:w], score[:, 0, 0:w], row_inv[:, 0:1], score[:, 1, 0:w],
                                         ALU.mult, ALU.subtract).then_inc(flag("wgt_done"), 1)
            elif name == "s_score":
                b = take(name, it)
                dve.tensor_reduce(s_stat[:, 0:1], M[b][0:16, 0, 0:CP], AX.X, ALU.max).then_inc(flag("s_raw_max"), 1)
                dve.wait_ge(flag("s_raw_max"), n)
                dve.tensor_scalar(s_stat[:, 1:2], s_stat[:, 0:1], -SCALE, None, ALU.mult).then_inc(flag("s_max_done"), 1)
                dve.wait_ge(*read(name, it))
                dve.reciprocal(s_stat[:, 3:4], s_stat[:, 2:3]).then_inc(flag("s_inv"), 1)
                dve.wait_ge(flag("s_inv"), n)
                dve.tensor_tensor(s_stat[:, 4:5], s_stat[:, 3:4], coef[:, :], ALU.mult).then_inc(flag("s_coef"), 1)
                dve.wait_ge(flag("s_coef"), n)
                dve.tensor_scalar(s_p[:, :], s_p[:, :], s_stat[:, 4:5], None, ALU.mult).then_inc(flag("s_p_done"), 1)
                dve.wait_ge(flag("s_p_done"), n)
                dve.tensor_scalar(new_w[0:16, :], K("pairs")[0:16, :], s_p[:, PAST:PAST + 1], None, ALU.mult).then_inc(flag("new_w_done"), 1)
            elif name == "s_prob":
                b = take(name, it)
                dve.tensor_reduce(w_sum[:, :], M[b][:, 0, 0:32].rearrange("p (x w) -> p x w", w=2), AX.X, ALU.add).then_inc(flag("w_sum_done"), 1)
                dve.tensor_copy(new_v[0:16, :], M[b][0:16, 1, 0:P]).then_inc(free[b], 1)
                dve.wait_ge(flag("w_sum_done"), n)
                wp = w_pad[:, :, :].rearrange("p (b g) c -> p b g c", g=PAGES)
                for g in range(PAGES):
                    t = dve.tensor_tensor(wp[:, :, g, :], w_sum[:, g * NS:(g + 1) * NS].unsqueeze(2).broadcast_to([P, NS, NS]),
                                          K("delta8").rearrange("p (b c) -> p b c", b=NS), ALU.mult)
                t.then_inc(flag("w_pad_done"), 1)
            elif name == "ssq_a":
                dve.wait_ge(flag("rr_a"), n)
                dve.scalar_tensor_tensor(mix_a[:, :], oT[:, :], gain_a[:, 0:1], rr[:, :], ALU.mult, ALU.mult).then_inc(flag("mix_a_done"), 1)
            elif name == "intra":
                b = take(name, it)
                dve.tensor_scalar(flat(intra[:, :, :]), M[b][:, 0, :], FINITE, -FINITE, ALU.min, ALU.max).then_inc(free[b], 1)
                dve.wait_ge(free[b], scratch.task(name, it)[1])
                dve.tensor_tensor(intra[:, :, :], intra[:, :, :],
                                  K("chunk_pairs").unsqueeze(1).broadcast_to([P, 4, P]), ALU.mult).then_inc(flag("intra_done"), 1)
            elif name.startswith("upd"):
                j = int(name[-1])
                b = take(name, it)
                for c in range(CPB):
                    x = j * CPB + c
                    u = M[b][:, c // 4, (c % 4) * P:(c % 4 + 1) * P]
                    dst = state[:, j % 2, c + 1, :] if c < CPB - 1 else state[:, (j + 1) % 2, 0, :]
                    if c == CPB - 1 and j > 0:
                        b2, v2 = scratch.task(f"rnn{j - 1}", it)
                        dve.wait_ge(full[b2], v2)
                    if x == 0:
                        t = dve.tensor_copy(dst, u)
                    else:
                        if c == 0:
                            dve.wait_ge(*read(f"upd{j - 1}", it))
                        else:
                            dve.wait_ge(flag("state_done"), r * 28 + (j * 7 + c))
                        t = dve.scalar_tensor_tensor(dst, state[:, j % 2, c, :], r_e[:, x * CHUNK + CHUNK - 1:x * CHUNK + CHUNK], u, ALU.mult, ALU.add)
                    if c < CPB - 1:
                        t.then_inc(flag("state_done"), 1)
                    else:
                        t.then_inc(free[b], 1)
                if j == 3:
                    dve.wait_ge(*read("i_nat", it))
                    dve.tensor_tensor(s_iexp[:, :, :], i_nat[0:NS, 4:5, :].broadcast_to([NS, NS, P]),
                                      K("delta_p")[0:NS, :].unsqueeze(2).broadcast_to([NS, NS, P]), ALU.mult).then_inc(flag("s_iexp_done"), 1)
            elif name == "s_upd":
                b = take(name, it, [("f_s_done", m), ("s_state_in", r * 16 + 16)])
                for y in range(NS):
                    t = dve.scalar_tensor_tensor(s_state[:, y, :], s_state[:, y, :], f_s[:, y:y + 1],
                                                 M[b][:, y // 4, (y % 4) * P:(y % 4 + 1) * P], ALU.mult, ALU.add)
                t.then_inc(free[b], 1)
            elif name == "late_ssq_r":
                dve.wait_ge(flag("rr_r"), m)
                dve.scalar_tensor_tensor(r_o[:, :], r_o[:, :], vec(ROWS_A["rnn"]), rr[:, :], ALU.mult, ALU.mult).then_inc(flag("r_normed"), 1)
                dve.wait_ge(flag("r_normed"), m)
                dve.wait_ge(flag("r_gate"), m)
                dve.tensor_tensor(mix_r[:, :], r_o[:, :], z_g[:, :], ALU.mult).then_inc(flag("mix_r_done"), 1)

        def step(plan, it, h, r):
            for s in range(HALVES):
                if h is not None and s % 4 == 0 and s > 0:
                    name = BLOCKS[s // 4 - 1]
                    evacuate(name, h, {"q": z_q, "k": z_k, "v": z_v, "f": z_f, "i": z_i, "r": z_r}[name])
                if r is not None and s == 0:
                    evacuate("g", r, z_g)
                if h is None and s % 2 == 0 and s > 0:
                    out_sum(s // 2 - 1)
                if h is None and s == 0:
                    for k in range(4):
                        mixed(k, xT[:, k, :])
                if s % 2 == 0 and (r is not None or s >= 2 * EARLY_CHUNKS - 2):
                    j = s // 2 + 1
                    low((HEADS if h is None else h) * HEAD_CHUNKS + j, j % 2)
                if r is not None and s == 0:
                    small("ssq_a", it, r, None)
                for name in late_parts(plan, s):
                    small(name, it, h, r)
                if h is None and s == 0:
                    for k in range(4, HEADS - 1):
                        mixed(k, xT[:, k, :])
                    mixed(HEADS - 1, mix_a[:, :])
                if h is None and s % 2 == 0 and 2 <= s < 2 * HEADS:
                    k = HEADS + s // 2 - 1
                    mixed(k, xT[:, k, :])
                if h is None and s == 24:
                    mixed(KT - 1, mix_r[:, :])
                if r is not None and s == 0:
                    dve.wait_ge(flag("sig_f"), r + 1)
                    dve.tensor_scalar(z_f[:, :], z_f[:, :], oml[:, bass.ds(r, 1)], lb[:, bass.ds(r, 1)], ALU.mult, ALU.add).then_inc(flag("f_done"), 1)
                    dve.wait_ge(flag("f_done"), r + 1)
                    dve.tensor_copy(f_s[:, :], z_f[:, SEQ:T]).then_inc(flag("f_s_done"), 1)
                    dve.tensor_scalar(r_k[:, :], r_k[:, :], oml[:, bass.ds(r, 1)], None, ALU.mult).then_inc(flag("r_k_done"), 1)
                    dve.wait_ge(flag("sig_g"), r + 1)
                    dve.tensor_tensor(z_g[:, :], z_g[:, :], r_g[:, :], ALU.mult).then_inc(flag("r_gate"), 1)
                    dve.wait_ge(flag("log_f"), r + 1)
                    dve.tensor_tensor_scan(r_b[:, :], K("restart"), r_kh[:, :], 0.0, ALU.mult, ALU.add).then_inc(flag("scan_done"), 1)
                    dve.wait_ge(flag("scan_done"), r + 1)
                    rb = r_b[:, :].rearrange("p (c t) -> p c t", t=CHUNK)
                    dve.tensor_tensor(r_kh[:, :].rearrange("p (c t) -> p c t", t=CHUNK),
                                      rb[:, :, CHUNK - 1:CHUNK].broadcast_to([P, NCH, CHUNK]), rb, ALU.subtract).then_inc(flag("b_left"), 1)
                for name in plan[s]:
                    if name != "ssq_a":
                        small(name, it, h, r)
            if r is not None and h is not None:
                dve.wait_ge(flag("state_out"), r * 16 + 16)
                dve.wait_ge(flag("mix_r_out"), r * 16 + 16)

        def mixed(k, src):
            dve.wait_ge(flag("act_hi_ready"), KT + k + 1)
            dve.tensor_tensor(act_lo[:, k, :], src, act_hi[:, k, :].bitcast(F32), ALU.subtract).then_inc(flag("act_lo_ready"), 1)

        def out_sum(n):
            dve.wait_ge(w_used, C_OUT + n + 1)
            dve.wait_ge(flag(f"x_back{n}"), 16)
            dve.tensor_tensor(two(xT[:, n, :]), G[n % 2][:, :, 0:TH], two(xT[:, n, :]), ALU.add).then_inc(g_free[n % 2], 1)

        def operand(k, src, gain, n):
            dve.wait_ge(flag("act_hi_ready"), n)
            dve.scalar_tensor_tensor(act_lo[:, k, :], src, gain, act_hi[:, k, :].bitcast(F32), ALU.mult, ALU.subtract).then_inc(flag("act_lo_ready"), 1)

        def add_squares(n, slot):
            dve.wait_ge(flag("squares"), n + 1)
            if not isinstance(n, int) or n > 0:
                dve.wait_ge(flag("sq_sum_done"), n)
            dve.tensor_tensor(sq_sum[:, :], sq_sum[:, :], sqx[:, slot, :], ALU.add).then_inc(flag("sq_sum_done"), 1)

        def zero_sum(n):
            dve.memset(sq_sum[:, :], 0.0).then_inc(flag("sum_zeroed"), 1)
            dve.wait_ge(flag("sum_zeroed"), n)

        def pad(it):
            if scratch.padded:
                b = take("pad", it)
                dve.tensor_copy(pad_out[:, :], M[b][0:32, 0, 0:1]).then_inc(free[b], 1)

        def visit(what, arg):
            if what == "early":
                b = take("rows_a", 0)
                dve.tensor_copy(vecs[:, 0:NROWS_A], M[b][:, 0, 0:NROWS_A]).then_inc(free[b], 1)
                b = take("rows_b", 0)
                dve.tensor_copy(vecs[:, NROWS_A:NCOLS], M[b][:, 0, 0:4 * FB]).then_inc(free[b], 1)
                dve.wait_ge(*read("rows_a", 0))
                dve.wait_ge(*read("rows_b", 0))
                for t in range(4):
                    b = take(f"x{t}1", 0)
                    dve.tensor_copy(xT0[:, 8:16, t * P:(t + 1) * P], M[b][:, :, :].rearrange("p a (y c) -> p (a y) c", y=4)).then_inc(free[b], 1)
                    if t == 2:
                        low(0, 0)
                dve.wait_ge(*read("x31", 0))
                for k in range(KT):
                    operand(k, xT0[:, k, :], vec(ROWS_A["norm_mix"] + k), k + 1)
                    if k in EARLY_SPLITS:
                        low(EARLY_SPLITS[k], EARLY_SPLITS[k] % 2)
                dve.wait_ge(flag("pool_sum"), 2 * POOL_TILES - 1)
                for k in range(SUM_EARLY):
                    add_squares(k, k % 2)
                    if k == KT // 2 - 1:
                        low(3, 1)
                dve.wait_ge(flag("xT_written"), 16)
                dve.wait_ge(flag("tables_in"), 16)
                dve.wait_ge(flag("lam_in"), 64)
                for i in range(2):
                    dve.tensor_tensor_reduce(lamv[:, 2 * i, :], lamv[:, 2 * i, :], lamv[:, 2 * i + 1, :], 1.0, 0.0,
                                             ALU.mult, ALU.add, lams[:, i:i + 1]).then_inc(flag("setup_a"), 1)
                rows = [vec(ROWS_A[x], HEADS) for x in ("lb0", "lb1")]
                dve.tensor_tensor(lbt[:, 2, :], rows[0], rows[1], ALU.max).then_inc(flag("lb_max"), 1)
                dve.wait_ge(flag("lb_max"), 1)
                for i in range(2):
                    dve.tensor_tensor(lbt[:, i, :], rows[i], lbt[:, 2, :], ALU.subtract).then_inc(flag("setup_a"), 1)
                dve.wait_ge(flag("setup_e"), 2)
                dve.tensor_tensor(lam[:, :], lams[:, 2:3], lams[:, 3:4], ALU.subtract).then_inc(flag("setup_d"), 1)
                dve.wait_ge(flag("setup_d"), 1)
                dve.tensor_scalar(lam[:, :], lam[:, :], LAM_INIT, None, ALU.add).then_inc(flag("setup_d"), 1)
                dve.wait_ge(flag("setup_d"), 2)
                dve.scalar_tensor_tensor(coef[:, :], K("coef")[0:16, 1:2], lam[0:16, 0:1], K("coef")[0:16, 0:1], ALU.mult, ALU.add).then_inc(flag("setup_d"), 1)
                dve.tensor_tensor(lbt[:, 2, :], lbt[:, 0, :], lbt[:, 1, :], ALU.add).then_inc(flag("setup_d"), 1)
                dve.wait_ge(flag("setup_d"), 4)
                dve.reciprocal(lbt[:, 1, :], lbt[:, 2, :]).then_inc(flag("setup_d"), 1)
                dve.wait_ge(flag("setup_d"), 5)
                dve.tensor_tensor(lb[:, :], lbt[:, 0, :], lbt[:, 1, :], ALU.mult).then_inc(flag("setup_d"), 1)
                dve.wait_ge(flag("setup_d"), 6)
                dve.tensor_scalar(oml[:, :], lb[:, :], -1.0, 1.0, ALU.mult, ALU.add).then_inc(flag("setup_d"), 1)
                dve.tensor_scalar(gain_a[:, :], vec(ROWS_A["att"]), 1.0 - LAM_INIT, None, ALU.mult).then_inc(flag("setup_d"), 1)
                dve.wait_ge(flag("setup_d"), 8)
                dve.wait_ge(flag("R_ready"), 1)
                dve.wait_ge(flag("zeros_set"), 2)
            elif what == "heads":
                plan, h0, h1 = arg
                if h0 == 0:
                    step(plan, 0, 0, None)
                elif h1 == HEADS:
                    with dve.Fori(h0, h1) as h:
                        step(plan, h - 1, h, h - 1)
                else:
                    step(plan, 0, None, HEADS - 1)
            elif what == "out":
                for n in range(HALVES // 2 - 1, KT):
                    out_sum(n)
                    low(C_OUT + n + 2, n % 2)
                zero_sum(1)

                def out_product(it, x):
                    dve.wait_ge(w_used, it * 2 + (C_RNN + x + 1))
                    dve.wait_ge(g_free[x], it + g_rnn[x])
                    dve.tensor_tensor(two(column(xT, it * 2 + x)), G[x][:, :, 0:TH], two(column(xT, it * 2 + x)), ALU.add).then_inc(g_free[x], 1)
                    low(it * 2 + (C_RNN + x + 2), x)
                    add_squares(it * 2 + (SUM_EARLY + x), x)
                with dve.Fori(0, KT // 4) as it:
                    for x in range(2):
                        out_product(it, x)
                dve.wait_ge(flag("pT_hi_done"), 1)
                dve.tensor_tensor(pT_lo[:, :, :], pT[:, :, :], pT_hi[:, :, :].bitcast(F32), ALU.subtract).then_inc(flag("pT_lo_done"), 1)
                with dve.Fori(KT // 4, KT // 2) as it:
                    for x in range(2):
                        out_product(it, x)
                pad(0)
                for k in range(KT):
                    operand(k, xT[:, k, :], vec(ROWS_A["norm_ffn"] + k), 2 * KT + k + 1)
                dve.wait_ge(flag("R_ready"), 2)
            elif what == "ffn":
                dve.memset(ffg[:, 0:2], 0.0).then_inc(flag("conv_zero"), 1)
                dve.wait_ge(flag("conv_zero"), 1)
                with dve.Fori(0, GROUPS) as g:
                    with dve.Fori(0, GF) as f:
                        n = g * GF + f
                        c0 = g * GROUP_CHUNKS + f * 4

                        def w(i):
                            return vecs[:, bass.ds(n + COL_CW[i], 1)]

                        def linked(ins, v):
                            ins.then_inc(flag("ff_step"), 1)
                            dve.wait_ge(flag("ff_step"), n * FF_STEPS + v)
                        low(c0 + (C_FFN + 2), 0)
                        dve.wait_ge(w_used, c0 + (C_FFN + 2))
                        b, v = scratch.task("c_new", n)
                        dve.wait_ge(full[b], v - 1)
                        dve.tensor_tensor(two(ffg[:, 2:T + 2]), G[0][:, :, 0:TH], two(R[:, :]), ALU.mult).then_inc(g_free[0], 1)
                        low(c0 + (C_FFN + 3), 1)
                        dve.wait_ge(g_free[0], g * g_per_group + f + (g_ffn[0] + 1))
                        linked(dve.tensor_scalar(ffc[:, :], ffg[:, 2:T + 2], w(2), w(3), ALU.mult, ALU.add), 1)
                        linked(dve.scalar_tensor_tensor(ffc[:, 0:SEQ], ffg[:, 1:SEQ + 1], w(1), ffc[:, 0:SEQ], ALU.mult, ALU.add), 2)
                        linked(dve.scalar_tensor_tensor(ffc[:, 0:SEQ], ffg[:, 0:SEQ], w(0), ffc[:, 0:SEQ], ALU.mult, ALU.add), 3)
                        cb, cv = scratch.task("c_old", g)
                        dve.wait_ge(free[cb], cv)
                        old = conv_old[:, bass.ds(f, 1), :, :].rearrange("p f b w -> p (f b) w")
                        past = [old[:, :, i:i + 1].rearrange("p b o -> p (b o)") for i in range(2)]
                        linked(dve.scalar_tensor_tensor(ffc[:, SEQ:T], past[1], w(1), ffc[:, SEQ:T], ALU.mult, ALU.add), 4)
                        dve.scalar_tensor_tensor(ffc[:, SEQ:T], past[0], w(0), ffc[:, SEQ:T], ALU.mult, ALU.add).then_inc(flag("ffc_done"), 1)
                        low(c0 + (C_FFN + 4), 0)
                        dve.wait_ge(w_used, c0 + (C_FFN + 4))
                        dve.tensor_tensor(two(ffu[:, :]), G[1][:, :, 0:TH], two(R[:, :]), ALU.mult).then_inc(g_free[1], 1)
                        low(c0 + (C_FFN + 5), 1)
                        dve.wait_ge(g_free[1], g * g_per_group + f + (g_ffn[1] + 1))
                        dve.wait_ge(flag("silu_done"), n + 1)
                        dve.tensor_tensor(ffu[:, :], ffu[:, :], ffs[:, :], ALU.mult).then_inc(flag("ffu_done"), 1)
                        dve.wait_ge(flag("u_hi_done"), n + 1)
                        dve.tensor_tensor(column(u_lo, f), ffu[:, :], column(u_hi, f).bitcast(F32), ALU.subtract).then_inc(flag("u_done"), 1)
                    dve.memset(sq_sum[:, :], 0.0).then_inc(flag("sum_zeroed"), 1)
                    with dve.Fori(0, KT // 2) as m:
                        for x in range(2):
                            c0 = g * GROUP_CHUNKS + m * 4
                            low(c0 + (C_FFN + FF_CHUNKS + 2 * x + 2), 0)
                            dve.wait_ge(w_used, c0 + (C_FFN + FF_CHUNKS + 2 * x + 2))
                            col = column(xT, m * 2 + x)
                            dve.tensor_tensor(two(col), G[x][:, :, 0:TH], two(col), ALU.add).then_inc(g_free[x], 1)
                            low(c0 + (C_FFN + FF_CHUNKS + 2 * x + 3), 1)
                            dve.wait_ge(flag("sum_zeroed"), g + 2)
                            add_squares(g * KT + m * 2 + (SUM_EARLY + KT + x), x)
            elif what == "mid":
                pad(0)
                for k in range(KT):
                    operand(k, xT[:, k, :], vec(ROWS_A["norm_ple"] + k), 3 * KT + k + 1)
                dve.wait_ge(flag("R_ready"), 3)
            elif what == "ple":
                def ple(m, x, last=False):
                    n = m * 2 + x
                    c = C_PLE + 3 * x
                    low(m * 6 + (c + 2), x % 2, GATE_TILES)
                    if not last:
                        low(m * 6 + (c + 3), (x + 1) % 2, GATE_TILES)
                    dve.wait_ge(w_used, m * 6 + (c + 3))
                    dve.tensor_tensor(two(gate[:, :]), G[x][:, :, 0:TH], two(R[:, :]), ALU.mult).then_inc(g_free[x], 1)
                    if not last:
                        low(m * 6 + (c + 4), x % 2, GATE_TILES)
                    b = take(f"pp{x}", m)
                    dve.wait_ge(flag("gate_done"), n + 1)
                    dve.tensor_tensor(two(gate[:, :]), m_wide(b), two(gate[:, :]), ALU.mult).then_inc(free[b], 1)
                    dve.wait_ge(free[b], scratch.task(f"pp{x}", m)[1])
                    if not isinstance(m, int) or m > 0:
                        b, v = scratch.task(f"y{x}", m)
                        dve.wait_ge(full[b], v - 2)
                    dve.tensor_tensor(y_t[:, x, :], column(xT, n), gate[:, :], ALU.add).then_inc(flag("y_done"), 1)

                ple(0, 0)
                ple(0, 1)
                with dve.Fori(1, KT // 2 - 1) as m:
                    for x in range(2):
                        ple(m, x)
                ple(KT // 2 - 1, 0)
                ple(KT // 2 - 1, 1, last=True)

        phases(visit)

    @block.gpsimd
    def _(pool):
        def step(plan, it, h, r):
            if r is None:
                return
            pool.wait_ge(flag("exp_nb"), r + 1)
            pool.wait_ge(flag("r_k_done"), r + 1)
            nc.gpsimd.tensor_tensor(r_kd[:, :], r_k[:, 0:SEQ], r_kd[:, :], ALU.mult).then_inc(flag("r_kd_done"), 1)
            nc.gpsimd.tensor_tensor(r_qd, z_r[:, 0:SEQ], r_e[:, :], ALU.mult).then_inc(flag("r_qd_done"), 1)
            pool.wait_ge(flag("exp_left"), r + 1)
            nc.gpsimd.tensor_tensor(r_kh[:, :], r_k[:, 0:SEQ], r_kh[:, :], ALU.mult).then_inc(flag("r_kh_done"), 1)
            pool.wait_ge(flag("i_nat_done"), r + 1)
            for j in range(4):
                if j > 0:
                    b, v = scratch.task(f"upd{j - 1}", it)
                    pool.wait_ge(full[b], v)
                nc.gpsimd.tensor_tensor(v_chunks[:, :, :], i_nat[:, j:j + 1, :].broadcast_to([P, CPB, P]),
                                        K("chunk_of").unsqueeze(2).broadcast_to([P, CPB, P]), ALU.mult).then_inc(flag("v_chunks_done"), 1)

        def visit(what, arg):
            if what == "early":
                for name in ("xs", "x31", "x30"):
                    pool.wait_ge(*read(name, 0))
                for i in range(POOL_TILES):
                    x = xT0[:, SUM_EARLY + i, :]
                    dst = sq_sum if i == 0 else sq_pool
                    if i > 0:
                        pool.wait_ge(flag("pool_sum"), 2 * i - 1)
                    nc.gpsimd.tensor_tensor(dst[:, :], x, x, ALU.mult).then_inc(flag("pool_sum"), 1)
                    if i > 0:
                        pool.wait_ge(flag("pool_sum"), 2 * i)
                        nc.gpsimd.tensor_tensor(sq_sum[:, :], sq_sum[:, :], sq_pool[:, :], ALU.add).then_inc(flag("pool_sum"), 1)
                pool.wait_ge(flag("xT_written"), 16)
                pool.wait_ge(flag("act_lo_ready"), KT)
                pool.wait_ge(flag("sq_sum_done"), SUM_EARLY)
                pool.wait_ge(flag("tables_in"), 16)
                nc.gpsimd.memset(new_w[:, :], 0.0).then_inc(flag("zeros_set"), 1)
                nc.gpsimd.memset(new_v[:, :], 0.0).then_inc(flag("zeros_set"), 1)
            elif what == "heads":
                plan, h0, h1 = arg
                if h0 == 0:
                    return
                if h1 == HEADS:
                    with pool.Fori(h0, h1) as h:
                        step(plan, h - 1, h, h - 1)
                else:
                    step(plan, 0, None, HEADS - 1)

        phases(visit)

    ctx.close()


_INS = ["x_prompt", "x_sample", "p_prompt", "p_sample", "cache_k", "cache_v", "state_rnn", "state_ffn_conv", "page_table",
        "norm_mix", "w_in", "q_norm", "k_norm", "lam_q1", "lam_k1", "lam_q2", "lam_k2", "att_out_norm", "rnn_out_norm",
        "lower_bounds", "w_out", "norm_ffn", "w_gate", "w_up", "conv_w", "conv_b", "w_down", "norm_ple", "w_ple_gate",
        "w_ple_proj"]
_OUTS = {
    "y_prompt": (1, SEQ, D),
    "y_sample": (NS, 1, D),
    "k_prompt": (1, 1, SEQ // PAGE, PAGE, HEADS, P),
    "v_prompt": (1, 1, SEQ // PAGE, PAGE, HEADS, P),
    "rnn_prompt": (1, 1, HEADS, P, P),
    "conv_prompt": (1, 1, 2, D_FF),
    "k_sample": (1, NS, 1, HEADS, P),
    "v_sample": (1, NS, 1, HEADS, P),
    "rnn_sample": (1, NS, HEADS, P, P),
    "conv_sample": (1, NS, 2, D_FF),
}


def kernel(**inputs):
    import concourse.bacc as bacc
    from concourse.bass_utils import run_bass_kernel_spmd as run

    nc = bacc.Bacc("TRN2", target_bir_lowering=False, num_devices=1)
    arrays, a, o = {}, {}, {}
    for name in _INS + ["consts"]:
        x = constants() if name == "consts" else np.ascontiguousarray(inputs[name])
        arrays[f"in_{name}"] = x
        a[name] = nc.dram_tensor(f"in_{name}", x.shape, mybir.dt.from_np(x.dtype), kind="ExternalInput").ap()
    for name, shape in _OUTS.items():
        o[name] = nc.dram_tensor(f"out_{name}", shape, F32, kind="ExternalOutput").ap()
    program(nc, a, o)
    r = run(nc, [arrays], core_ids=[0])
    return tuple(r.results[0][f"out_{name}"] for name in _OUTS)
```
